# Optimizing a Trainium2 kernel written in Bass

```python
import math
import jax, jax.numpy as jnp
from jax import lax
import numpy as np

D_MODEL = 2048
BATCH = 1
SEQ = 256
DEPTH = 1

CHUNK = 64
Q_BLOCK = 128
MIX_WIDTH = D_MODEL
MLA_HEADS = 8
MLA_Q_RANK = 512
MLA_KV_RANK = 256
MLA_NOPE_DIM = 128
MLA_ROPE_DIM = 64
MLA_V_DIM = 128
FOX_HEADS = 8
FOX_HEAD_DIM = 128
D_FF = 5632
MACARON_WEIGHT = 0.5
ROPE_THETA = 10000.0
EPS = 1e-6
N_MOD = 9
FOX_WIDTH = FOX_HEADS * FOX_HEAD_DIM
IN_SIZES = (MLA_Q_RANK, MLA_KV_RANK, MLA_ROPE_DIM, FOX_WIDTH, FOX_WIDTH, FOX_WIDTH, FOX_HEADS)
IN_WIDTH = sum(IN_SIZES)
IN_OFFSETS = tuple(int(v) for v in np.cumsum(IN_SIZES)[:-1])

kernel_name = "hybrid_mla_fox_macaron_adaln_block"

def rmsnorm(x, g):
    xf = x.astype(jnp.float32)
    xf = xf * lax.rsqrt(jnp.mean(xf * xf, axis=-1, keepdims=True) + EPS)
    return xf.astype(x.dtype) * g

def modulate(h, shift, scale):
    return h * (1 + scale[:, None, :]) + shift[:, None, :]

def swiglu(h, w_gate, w_up, w_down):
    return (jax.nn.silu(h @ w_gate) * (h @ w_up)) @ w_down

def rotary(x, pos):
    half = x.shape[-1] // 2
    inv = ROPE_THETA ** (-jnp.arange(half, dtype=jnp.float32) / half)
    ang = pos.astype(jnp.float32)[:, None] * inv[None, :]
    cos = jnp.cos(ang)[None, :, None, :].astype(x.dtype)
    sin = jnp.sin(ang)[None, :, None, :].astype(x.dtype)
    x1, x2 = x[..., :half], x[..., half:]
    return jnp.concatenate([x1 * cos - x2 * sin, x1 * sin + x2 * cos], axis=-1)

def blocked_attention(q, k, v, scale, logit_fn):
    S = q.shape[1]
    outs = []
    for i in range(S // Q_BLOCK):
        q0 = i * Q_BLOCK
        kv_len = q0 + Q_BLOCK
        s = jnp.einsum('bqhd,bkhd->bhqk', q[:, q0:kv_len], k[:, :kv_len]).astype(jnp.float32) * scale
        p = jax.nn.softmax(logit_fn(s, q0, kv_len), axis=-1)
        outs.append(jnp.einsum('bhqk,bkhd->bqhd', p.astype(v.dtype), v[:, :kv_len]))
    return jnp.concatenate(outs, axis=1)

def chunk_causal_logits(s, q0, kv_len):
    t = q0 + jnp.arange(Q_BLOCK)
    src = jnp.arange(kv_len)
    mask = (src[None, :] // CHUNK) <= (t[:, None] // CHUNK)
    return jnp.where(mask[None, None], s, -jnp.inf)

def hybrid_mixer(h, pos, w_in, b_forget, g_q_a, w_uq, g_kv_a, w_ukv, w_o):
    B, S, _ = h.shape
    proj = h @ w_in
    q_a, kv_a, k_pe, fq, fk, fv, f_logit = jnp.split(proj, IN_OFFSETS, axis=-1)

    q = (rmsnorm(q_a, g_q_a) @ w_uq).reshape(B, S, MLA_HEADS, MLA_NOPE_DIM + MLA_ROPE_DIM)
    kv = (rmsnorm(kv_a, g_kv_a) @ w_ukv).reshape(B, S, MLA_HEADS, MLA_NOPE_DIM + MLA_V_DIM)
    k_nope, v_mla = kv[..., :MLA_NOPE_DIM], kv[..., MLA_NOPE_DIM:]
    q_mla = jnp.concatenate([q[..., :MLA_NOPE_DIM], rotary(q[..., MLA_NOPE_DIM:], pos)], axis=-1)
    k_rope = rotary(k_pe[:, :, None, :], pos)
    k_mla = jnp.concatenate(
        [k_nope, jnp.broadcast_to(k_rope, (B, S, MLA_HEADS, MLA_ROPE_DIM))], axis=-1)
    o_mla = blocked_attention(q_mla, k_mla, v_mla,
                              1.0 / math.sqrt(MLA_NOPE_DIM + MLA_ROPE_DIM), chunk_causal_logits)

    log_f = jax.nn.log_sigmoid((f_logit + b_forget).astype(jnp.float32))
    cum = jnp.cumsum(log_f, axis=1).transpose(0, 2, 1)

    def fox_logits(s, q0, kv_len):
        bias = cum[:, :, q0:kv_len, None] - cum[:, :, None, :kv_len]
        t = q0 + jnp.arange(Q_BLOCK)
        mask = jnp.arange(kv_len)[None, :] <= t[:, None]
        return jnp.where(mask[None, None], s + bias, -jnp.inf)

    o_fox = blocked_attention(fq.reshape(B, S, FOX_HEADS, FOX_HEAD_DIM),
                              fk.reshape(B, S, FOX_HEADS, FOX_HEAD_DIM),
                              fv.reshape(B, S, FOX_HEADS, FOX_HEAD_DIM),
                              1.0 / math.sqrt(FOX_HEAD_DIM), fox_logits)

    o = jnp.concatenate([o_mla.reshape(B, S, MLA_HEADS * MLA_V_DIM),
                         o_fox.reshape(B, S, FOX_WIDTH)], axis=-1)
    return o @ w_o

def setup_inputs(seed: int = 0) -> dict:
    key = jax.random.key(seed)
    ks = jax.random.split(key, 32)
    f32 = jnp.float32
    L, D = DEPTH, D_MODEL

    def w(k, shape, fan_in, mult=1.0):
        return jax.random.normal(k, shape, f32) * (mult * fan_in ** -0.5)

    def gain(k, dim):
        return 1.0 + 0.05 * jax.random.normal(k, (L, dim), f32)

    return {
        "x": jax.random.normal(ks[0], (BATCH, SEQ, D), f32),
        "c": jax.random.normal(ks[1], (BATCH, D), f32),
        "w_ada": w(ks[2], (L, D, N_MOD * D), D, 0.5),
        "b_ada": 0.02 * jax.random.normal(ks[3], (L, N_MOD * D), f32),
        "g_ffn1_pre": gain(ks[4], D),
        "g_ffn1_post": gain(ks[5], D),
        "w1_gate": w(ks[6], (L, D, D_FF), D),
        "w1_up": w(ks[7], (L, D, D_FF), D),
        "w1_down": w(ks[8], (L, D_FF, D), D_FF),
        "g_mix_pre": gain(ks[9], D),
        "g_mix_post": gain(ks[10], D),
        "w_in": w(ks[11], (L, D, IN_WIDTH), D),
        "b_forget": jax.random.uniform(ks[12], (L, FOX_HEADS), f32, 1.0, 4.0),
        "g_q_a": gain(ks[13], MLA_Q_RANK),
        "w_uq": w(ks[14], (L, MLA_Q_RANK, MLA_HEADS * (MLA_NOPE_DIM + MLA_ROPE_DIM)), MLA_Q_RANK),
        "g_kv_a": gain(ks[15], MLA_KV_RANK),
        "w_ukv": w(ks[16], (L, MLA_KV_RANK, MLA_HEADS * (MLA_NOPE_DIM + MLA_V_DIM)), MLA_KV_RANK),
        "w_o": w(ks[17], (L, MIX_WIDTH, D), MIX_WIDTH),
        "g_ffn2_pre": gain(ks[18], D),
        "g_ffn2_post": gain(ks[19], D),
        "w2_gate": w(ks[20], (L, D, D_FF), D),
        "w2_up": w(ks[21], (L, D, D_FF), D),
        "w2_down": w(ks[22], (L, D_FF, D), D_FF),
    }

def reference(x, c, w_ada, b_ada, g_ffn1_pre, g_ffn1_post, w1_gate, w1_up, w1_down,
              g_mix_pre, g_mix_post, w_in, b_forget, g_q_a, w_uq, g_kv_a, w_ukv, w_o,
              g_ffn2_pre, g_ffn2_post, w2_gate, w2_up, w2_down):
    pos = jnp.arange(x.shape[1])
    cond = jax.nn.silu(c)
    for l in range(DEPTH):
        mod = cond @ w_ada[l] + b_ada[l]
        sh1, sc1, gt1, sh2, sc2, gt2, sh3, sc3, gt3 = jnp.split(mod, N_MOD, axis=-1)
        h = modulate(rmsnorm(x, g_ffn1_pre[l]), sh1, sc1)
        y = rmsnorm(swiglu(h, w1_gate[l], w1_up[l], w1_down[l]), g_ffn1_post[l])
        x = x + MACARON_WEIGHT * gt1[:, None, :] * y
        h = modulate(rmsnorm(x, g_mix_pre[l]), sh2, sc2)
        y = hybrid_mixer(h, pos, w_in[l], b_forget[l], g_q_a[l], w_uq[l], g_kv_a[l], w_ukv[l], w_o[l])
        x = x + gt2[:, None, :] * rmsnorm(y, g_mix_post[l])
        h = modulate(rmsnorm(x, g_ffn2_pre[l]), sh3, sc3)
        y = rmsnorm(swiglu(h, w2_gate[l], w2_up[l], w2_down[l]), g_ffn2_post[l])
        x = x + MACARON_WEIGHT * gt3[:, None, :] * y
    return x


_drawn_inputs = setup_inputs


def setup_inputs(seed=0):
    import zlib

    import numpy as np

    out = dict(_drawn_inputs(seed))
    spreads = {}
    factors = {'g_ffn1_pre': 5.306,
     'g_ffn1_post': 6.992,
     'g_mix_pre': 3.447,
     'g_mix_post': 3.882,
     'g_q_a': 8.0,
     'g_kv_a': 6.447,
     'g_ffn2_pre': 5.647,
     'g_ffn2_post': 8.0}
    for name, (base, spread) in spreads.items():
        noise = np.random.default_rng([zlib.crc32(name.encode()), seed]).standard_normal(out[name].shape)
        drawn = base * np.exp(spread * noise) if base else spread * noise
        out[name] = __import__('jax').numpy.asarray(drawn.astype(out[name].dtype))
    for name, factor in factors.items():
        out[name] = (out[name] * factor).astype(out[name].dtype)
    return out
```

```python
from contextlib import ExitStack

import numpy as np

import concourse.bass as bass
from concourse import mybir

F32 = mybir.dt.float32
F32R = mybir.dt.float32r
BF16 = mybir.dt.bfloat16
ALU = mybir.AluOpType
ACT = mybir.ActivationFunctionType
AX_X = mybir.AxisListType.X

P = 128
SEQ = 256
TT = SEQ // P
D = 2048
KD = D // P
FF = 5632
Q_RANK, KV_RANK = 512, 256
NOPE, ROPE, DV = 128, 64, 128
HEADS = 8
CHUNK = 64
EPS = 1e-6
N_MOD = 9
IN_WIDTH = Q_RANK + KV_RANK + ROPE + 3 * HEADS * P + HEADS
NB = 512
FB = FF // NB
DB = D // NB
QK = NOPE + ROPE
MLA_SCALE = float(QK) ** -0.5
FOX_SCALE = float(P) ** -0.5
MASKED = -1e38

C_ID, C_TRI, C_ONE, C_MF, C_MM = 0, P, 2 * P, 3 * P, 4 * P
C_COS, C_SIN = 5 * P, 5 * P + TT * ROPE // 2
C_ALL = 5 * P + TT * ROPE
G_PRE = {"ffn1": 144, "mix": 176, "ffn2": 208}
G_POST = {"ffn1": 160, "mix": 192, "ffn2": 224}
G_QA, G_KV = 240, 244
V_ROWS = 246

RING = 4


def pattern(n_w, ada_after):
    seq = []
    for u in range(n_w):
        seq.append(("W", u))
        for _ in range(ada_after.count(u)):
            seq.append(("A", sum(k == "A" for k, _ in seq)))
    return seq


class Block:

    def __init__(self, at, seq, products, quarter):
        self.r, self.w, self.g, self.m = at["r"], at["w"], at["g"], at["m"]
        self.seq = seq
        self.nw = sum(k == "W" for k, _ in seq)
        self.na = len(seq) - self.nw
        self.q = at["q"] if self.na else None
        assert self.na == 8 * quarter
        at["r"] += len(seq)
        at["w"] += self.nw
        at["g"] += products
        at["m"] += bool(self.na)
        at["q"] += quarter
        self.w_end = at["w"]

    def r_of(self, u):
        return self.r + self.seq.index(("W", u))


def make_plan():
    at = dict(r=0, w=0, g=0, m=0, q=0)
    pl = {}
    pl["pre"] = [Block(at, pattern_ada(16), 0, 2) for _ in range(4)]
    gu_ada = pattern(16, [4, 5, 7, 8, 10, 11, 13, 14])
    gu = pattern(16, [])
    pl["gu1"] = [Block(at, gu_ada, 2, 1) for _ in range(FB)]
    pl["down1"] = [Block(at, pattern(22, list(range(5, 21))), 1, 2) for _ in range(DB)]
    win_ada = pattern(8, [3, 4, 4, 5, 5, 6, 6, 7])
    pl["win"] = [Block(at, win_ada if b in (0, 1, 6, 7) else pattern(8, []), 1, int(b in (0, 1, 6, 7)))
                 for b in range(8)]
    pl["uq"] = [Block(at, pattern(2, []), 1, 0) for _ in range(3)]
    pl["ukv"] = [Block(at, pattern(1, []), 1, 0) for _ in range(4)]
    pl["wo"] = [Block(at, win_ada, 1, 1) for _ in range(DB)]
    pl["gu2"] = [Block(at, gu_ada if b == 0 else gu, 2, int(b == 0)) for b in range(FB)]
    pl["down2"] = [Block(at, pattern(22, []), 1, 0) for _ in range(DB)]
    assert at["q"] == N_MOD * DB
    tp, owner = {}, []

    def fills(name, n, by):
        tp[name] = len(owner)
        owner.extend(by * n)

    for f in ("1", "2"):
        fills("mod" + f, 8, "v")
        fills("hid" + f, 2 * (FB - 1), "v")
        fills("gate" + f, 2, "a")
        fills("hidlast" + f, 2, "v")
        fills("gateb" + f, 2, "a")
        if f == "1":
            fills("modmix", 8, "v")
            fills("qa", 2, "v")
            fills("kv", 1, "v")
            fills("kpe", 1, "v")
            fills("fqk", 8, "v")
            fills("qn", 4, "a")
            fills("kn", 4, "v")
            fills("qr", 4, "v")
            fills("pt", 2 * HEADS, "a")
            fills("gatemix", 4, "a")
    taken = [(o, owner[:n + 1].count(o)) for n, o in enumerate(owner)]
    return pl, tp, taken


def pattern_ada(n):
    return [("A", a) for a in range(n)]


def build(nc, A, const, out):
    pl, tp, taken = make_plan()
    ctx = ExitStack()
    with ctx:
        def sb(name, shape, dt=F32):
            return ctx.enter_context(nc.sbuf_tensor(name, shape, dt))

        def sem(name):
            return ctx.enter_context(nc.semaphore(name))

        raw = sb("raw", [P, RING, 2, NB])
        w_hi = sb("w_hi", [P, RING, 2, NB], F32R)
        w_lo = sb("w_lo", [P, RING, 2, NB], F32R)
        x = sb("x", [P, TT, D])
        y = sb("y", [P, TT, D])
        s = sb("s", [P, TT, NB])
        acc = sb("acc", [P, 2, NB])
        tmp = sb("tmp", [P, 2, NB])
        cst = sb("cst", [P, C_ALL])
        msk = sb("msk", [P, 3, P], BF16)
        col = sb("col", [P, V_ROWS])
        mod = sb("mod", [P, N_MOD * KD])
        a_col = sb("a_col", [P, KD])
        g_col = sb("g_col", [P, KD])
        c_col = sb("c_col", [P, 2, KD])
        ssq = sb("ssq", [P, TT, DB])
        ms = sb("ms", [P, TT])
        inv_ms = sb("inv_ms", [P, TT])
        newton = sb("newton", [P, TT])
        rstd = sb("rstd", [P, TT])
        kpe = sb("kpe", [P, 2, TT, ROPE])
        fz = sb("fz", [P, 5, TT, HEADS])
        nmax = sb("nmax", [P, 2, TT])
        nbias = sb("nbias", [P, 2, TT])
        rsum = sb("rsum", [P, 2, TT])
        rinv = sb("rinv", [P, 2, TT])
        ident = cst[:, C_ID:C_ID + P]
        tri = cst[:, C_TRI:C_TRI + P]
        ones = cst[:, C_ONE:C_ONE + P]
        h_hi = sb("h_hi", [P, KD, SEQ], F32R)
        with nc.sbuf_tensor("gate_ffn", [P, D], F32) as gate_ffn:
            pass
        h_lo = sb("h_lo", [P, KD, SEQ], F32R)
        with ExitStack() as mix:
            def mx(name, shape, dt=F32):
                return mix.enter_context(nc.sbuf_tensor(name, shape, dt))
            qa_hi = mx("qa_hi", [P, Q_RANK // P, SEQ], F32R)
            qa_lo = mx("qa_lo", [P, Q_RANK // P, SEQ], F32R)
            ka_hi = mx("ka_hi", [P, KV_RANK // P, SEQ], F32R)
            ka_lo = mx("ka_lo", [P, KV_RANK // P, SEQ], F32R)
            fqk = mx("fqk", [P, 2 * HEADS, SEQ])
            fv = mx("fv", [P, TT, HEADS * P])
            kv = mx("kv", [P, TT, HEADS * (NOPE + DV)])
            qnT = mx("qnT", [P, HEADS, SEQ])
            knT = mx("knT", [P, HEADS, SEQ])
            qrT = mx("qrT", [P, HEADS, SEQ])
            krT = mx("krT", [P, SEQ])
            sel = mx("sel", [P, HEADS, P])
            cumT = mx("cumT", [P, SEQ])
            prob = mx("prob", [P, 2, 3 * P])
            probT = mx("probT", [P, 2, 3 * P])
        hid_hi = sb("hid_hi", [P, FF // P, SEQ], F32R)
        hid_lo = sb("hid_lo", [P, FF // P, SEQ], F32R)
        gate_mix = kv[:, 0, :]

        pair = [ctx.enter_context(nc.psum_tensor(f"pair{i}", [P, TT, NB], F32)) for i in range(2)]
        tps = ctx.enter_context(nc.psum_tensor("tps", [P, 2, NB], F32))
        mps = ctx.enter_context(nc.psum_tensor("mps", [P, 2, NB], F32))

        raw_landed = [sem(f"raw_landed{i}") for i in range(RING)]
        small_landed = sem("small_landed")
        x_landed = sem("x_landed")
        sel_landed = sem("sel_landed")
        out_stored = sem("out_stored")
        hi_ready = sem("hi_ready")
        raw_used = sem("raw_used")
        w_used = sem("w_used")
        evac = [sem(f"evac{i}") for i in range(2)]
        t_full = sem("t_full")
        t_taken = {"v": sem("t_taken_v"), "a": sem("t_taken_a")}
        t_hi = sem("t_hi")
        h_ready = sem("h_ready")
        sum_ready = sem("sum_ready")
        mod_ready = sem("mod_ready")
        dg_ready = sem("dg_ready")
        sq_ready = sem("sq_ready")
        ms_ready = sem("ms_ready")
        rstd_ready = sem("rstd_ready")
        x_ready = sem("x_ready")
        xn_ready = sem("xn_ready")
        cols_full = sem("cols_full")
        setup = sem("setup")
        c_ready = sem("c_ready")
        rot_ready = sem("rot_ready")
        fz_v = sem("fz_v")
        fz_a = sem("fz_a")
        cum_full = sem("cum_full")
        cum_ready = sem("cum_ready")
        score_full = sem("score_full")
        nbias_ready = sem("nbias_ready")
        exp_ready = sem("exp_ready")
        prob_ready = sem("prob_ready")
        o_full = sem("o_full")
        ohi_ready = sem("ohi_ready")
        o_ready = sem("o_ready")

        SMALL = 16 * 7
        doubled = [b_r for b_r in [pl["win"][1].r_of(u) for u in range(8)]]

        def landed(r, i=0, per=0):
            extra = sum(q <= r and q % RING == r % RING for q in doubled)
            return 16 * (r // RING + 1 + extra) + (i * (16 * per // RING) if per else 0)

        def plus(n, i, per):
            return n + i * per if per else n

        N_X0, N_Y1, N_X1, N_QA, N_KV, N_YM, N_XM, N_Y2 = range(8)
        SQ = {}
        n_sq = 0
        for k, n in ((N_X0, 8), (N_Y1, 8), (N_X1, 8), (N_QA, 2), (N_KV, 2), (N_YM, 8), (N_XM, 8), (N_Y2, 8)):
            SQ[k] = n_sq
            n_sq += n
        XN = {"ffn1": 0, "mix": 4, "ffn2": 8}
        HR = {"ffn1": 0, "mix": 8, "qa": 16, "kv": 18, "ffn2": 19}
        TH = {}
        n_th = 0
        for k, n in (("mod1", 8), ("hid1", 2 * FB), ("modmix", 8), ("qa", 2), ("kv", 1), ("mod2", 8), ("hid2", 2 * FB)):
            TH[k] = n_th
            n_th += n
        DG = {"ffn1": 0, "mix": 4, "ffn2": 8}
        N_ATT = 2 * HEADS

        block = ctx.enter_context(nc.Block())

        @block.sync
        def _(sp):
            ada = A["w_ada"].rearrange("(p j) n -> p j n", j=KD)

            def load(r, src, n=NB, i=0, per=0, more=None):
                if per or r >= RING:
                    sp.wait_ge(raw_used, plus(r - RING + 1, i, per))
                sp.dma_start(raw[:, r % RING, :, 0:n], src).then_inc(raw_landed[r % RING], 16)
                if more is not None:
                    sp.dma_start(raw[:, r % RING, :, n:n + more.shape[2]], more).then_inc(raw_landed[r % RING], 16)

            def stream(b, unit, i=0, per=0, per_q=0):
                for n, (kind, u) in enumerate(b.seq):
                    if kind == "W":
                        src, cols, more = unit(u)
                        load(b.r + n, src, cols, i, per, more)
                    else:
                        c0 = plus(b.q + u // 8, i, per_q) * NB
                        j = 2 * (u % 8)
                        load(b.r + n, ada[:, j:j + 2, bass.ds(c0, NB)], NB, i, per)

            def unit_of(w, cols, at):
                v = w.rearrange("(k p) n -> p k n", p=P)
                return lambda u: (v[:, 2 * u:2 * u + 2, bass.ds(at, cols)], cols, None)

            def gate_up(gate, up, cb):
                g, v = unit_of(gate, NB, cb * NB), unit_of(up, NB, cb * NB)
                return lambda u: g(u) if u < 8 else v(u - 8)

            for t in range(TT):
                sp.dma_start(x[:, t, :], A["x"][t * P:(t + 1) * P, :]).then_inc(x_landed, 16)
            stream(pl["pre"][0], None)
            with sp.Fori(0, 3) as i:
                stream(pl["pre"][1], None, i, 16, 2)

            for f, gu, down in (("1", "gu1", "down1"), ("2", "gu2", "down2")):
                wg, wu, wd = A[f"w{f}_gate"], A[f"w{f}_up"], A[f"w{f}_down"]
                first, second = pl[gu][0], pl[gu][1]
                stream(first, gate_up(wg, wu, 0))
                per = len(second.seq)
                with sp.Fori(0, FB - 1) as i:
                    stream(second, gate_up(wg, wu, i + 1), i, per, int(second.na > 0))
                b0, b1 = pl[down][0], pl[down][1]
                per = 2 * len(b0.seq)
                with sp.Fori(0, 2) as i:
                    stream(b0, unit_of(wd, NB, i * (2 * NB)), i, per, 4)
                    stream(b1, unit_of(wd, NB, i * (2 * NB) + NB), i, per, 4)
                if f == "2":
                    break
                w_in = A["w_in"]
                kv0 = Q_RANK
                kvn = KV_RANK + ROPE
                lg = w_in.rearrange("(k p) n -> p k n", p=P)
                for b in range(8):
                    if b == 1:
                        v = unit_of(w_in, kvn, kv0)
                        stream(pl["win"][1], lambda u: (v(u)[0], kvn, lg[:, 2 * u:2 * u + 2, IN_WIDTH - HEADS:IN_WIDTH]))
                        sp.wait_ge(w_used, pl["down1"][-1].w_end)
                        sp.dma_start(sel[:], const["sel"].rearrange("k (h p) -> k h p", h=HEADS)).then_inc(sel_landed, 16)
                    else:
                        at = 0 if b == 0 else Q_RANK + kvn + (b - 2) * NB
                        stream(pl["win"][b], unit_of(w_in, NB, at))
                for b in range(3):
                    stream(pl["uq"][b], unit_of(A["w_uq"], NB, b * NB))
                for b in range(4):
                    stream(pl["ukv"][b], unit_of(A["w_ukv"], NB, b * NB))
                b0, b1 = pl["wo"][0], pl["wo"][1]
                with sp.Fori(0, 2) as i:
                    stream(b0, unit_of(A["w_o"], NB, i * (2 * NB)), i, 2 * len(b0.seq), 2)
                    stream(b1, unit_of(A["w_o"], NB, i * (2 * NB) + NB), i, 2 * len(b0.seq), 2)

            for t in range(TT):
                sp.wait_ge(x_ready, 8 * 2 + 4 * (t + 1))
                sp.dma_start(out[t * P:(t + 1) * P, :], x[:, t, :]).then_inc(out_stored, 16)
            sp.wait_ge(out_stored, 16 * TT)

        @block.scalar
        def _(act):
            def hi_unit(b, u, i=0, per=0, per_w=0, n=NB):
                r, w = b.r_of(u), b.w + u
                act.wait_ge(raw_landed[r % RING], landed(r, i, per))
                if per or w >= RING:
                    act.wait_ge(w_used, plus(w - RING + 1, i, per_w))
                nc.scalar.activation(w_hi[:, w % RING, :, 0:n], raw[:, r % RING, :, 0:n], ACT.Copy).then_inc(hi_ready, 1)

            def square_x(k):
                for t in range(TT):
                    for b in range(DB):
                        n = 4 * t + b
                        if k == N_X0:
                            if n % 4 == 0:
                                act.wait_ge(x_landed, 16 * TT)
                        else:
                            act.wait_ge(x_ready, 8 * {N_X1: 0, N_XM: 1}[k] + n + 1)
                        act.drain()
                        nc.scalar.activation(s[:, t, :], x[:, t, b * NB:(b + 1) * NB], ACT.Square,
                                             accum_out=ssq[:, t, b:b + 1]).then_inc(sq_ready, 1)

            def root(k):
                act.wait_ge(ms_ready, k + 1)
                nc.scalar.activation(rstd[:], inv_ms[:], ACT.Sqrt).then_inc(rstd_ready, 1)

            def hi_mod(t0, dst, n_pieces, between=None):
                for cp in range(n_pieces):
                    if between is not None and cp in (2, 4, 6):
                        between(cp // 2 + 1)
                    act.wait_ge(t_taken["v"], taken[t0 + cp][1])
                    nc.scalar.activation(dst[:, 2 * cp:2 * cp + 2, :],
                                         tmp[:, cp % 2, :].rearrange("p (c t) -> p c t", c=2),
                                         ACT.Copy).then_inc(t_hi, 1)

            def silu(b, i=0, per_w=0, per_g=0, t_prev=None, per_t=0):
                act.wait_ge(w_used, plus(b.w + 8, i, per_w))
                if t_prev is not None:
                    act.wait_ge(t_full, plus(t_prev, i, per_t))
                for t in range(TT):
                    ins = nc.scalar.activation(s[:, t, :], pair[b.g % 2][:, t, :], ACT.Silu)
                ins.then_inc(evac[b.g % 2], 1)

            def hi_hid(t0, c0, i=0, per_t=0):
                for k in range(2):
                    act.wait_ge(t_full, plus(t0 + k + 1, i, per_t))
                    nc.scalar.activation(hid_hi[:, bass.ds(c0 + 2 * k, 2), :],
                                         tps[:, (t0 + k) % 2, :].rearrange("p (c t) -> p c t", c=2),
                                         ACT.Copy).then_inc(t_hi, 1)

            def gate_row(dst, t0, j0, n):
                for j in range(n):
                    act.wait_ge(t_full, t0 + j + 1)
                    nc.scalar.activation(dst[:, (j0 + j) * NB:(j0 + j + 1) * NB], tps[:, (t0 + j) % 2, :],
                                         ACT.Copy).then_inc(t_taken["a"], 1)

            def square_y(b, k, blk):
                act.wait_ge(w_used, b.w_end)
                act.drain()
                for t in range(TT):
                    nc.scalar.activation(s[:, t, :], pair[b.g % 2][:, t, :], ACT.Square,
                                         accum_out=ssq[:, t, blk:blk + 1]).then_inc(sq_ready, 1)

            act.dma_start(cst[:], const["cst"]).then_inc(small_landed, 16)
            act.dma_start(c_col[:, 0, :], A["c"].rearrange("o (p j) -> (o p) j", j=KD)).then_inc(small_landed, 16)
            act.dma_start(y[:, 0, 0:P], A["b_ada"].rearrange("(r c) -> r c", c=P)[0:P, :]).then_inc(small_landed, 16)
            act.dma_start(y[0:N_MOD * KD - P, 0, P:2 * P],
                          A["b_ada"].rearrange("(r c) -> r c", c=P)[P:, :]).then_inc(small_landed, 16)
            act.dma_start(y[N_MOD * KD - P:G_QA - P, 0, P:2 * P], const["gains"]).then_inc(small_landed, 16)
            act.dma_start(y[G_QA - P:V_ROWS - P, 0, P:2 * P], const["gains_a"]).then_inc(small_landed, 16)
            act.dma_start(fz[:, 0, 0, :], A["b_forget"].rearrange("(o h) -> o h", o=1).to_broadcast([P, HEADS])).then_inc(small_landed, 16)
            act.wait_ge(small_landed, SMALL)
            nc.scalar.activation(c_col[:, 1, :], c_col[:, 0, :], ACT.Silu).then_inc(c_ready, 1)
            square_x(N_X0)
            root(N_X0)

            for f, gu, down in (("1", "gu1", "down1"), ("2", "gu2", "down2")):
                first, second = pl[gu][0], pl[gu][1]
                per, t0 = len(second.seq), tp["hid" + f]
                hi_unit(first, 0)
                hi_unit(first, 1)
                if f == "2":
                    square_x(N_XM)
                    root(N_XM)
                hi_mod(tp["mod" + f], h_hi, 8, lambda u: hi_unit(first, u))
                for u in range(5, 16):
                    if u == 12:
                        silu(first)
                    hi_unit(first, u)
                with act.Fori(0, FB - 1) as i:
                    for u in range(16):
                        if u == 7:
                            hi_hid(t0, i * 4, i, 2)
                        if u == 12:
                            silu(second, i, 16, 1, t0 + 2, 2)
                        hi_unit(second, u, i, per, 16)
                b0 = pl[down][0]
                hi_unit(b0, 0)
                hi_unit(b0, 1)
                gate_row(gate_ffn, tp["gate" + f], 0, 2)
                hi_hid(tp["hidlast" + f], 4 * (FB - 1))
                gate_row(gate_ffn, tp["gateb" + f], 2, 2)
                k_y = N_Y1 if f == "1" else N_Y2
                for n, b in enumerate(pl[down]):
                    for u in range(22):
                        if n == 0 and u < 2:
                            continue
                        if u == 4 and n:
                            square_y(pl[down][n - 1], k_y, n - 1)
                        hi_unit(b, u)
                square_y(pl[down][-1], k_y, DB - 1)
                root(k_y)
                if f == "2":
                    break

                win = pl["win"]
                hi_unit(win[0], 0)
                hi_unit(win[0], 1)
                square_x(N_X1)
                root(N_X1)
                hi_mod(tp["modmix"], h_hi, 8, lambda u: hi_unit(win[0], u))
                for u in range(5, 8):
                    hi_unit(win[0], u)

                def stage(b, dst):
                    act.wait_ge(w_used, b.w_end)
                    for t in range(TT):
                        ins = nc.scalar.activation(dst(t), pair[b.g % 2][:, t, :], ACT.Copy)
                    ins.then_inc(evac[b.g % 2], 1)

                def small_squares(b, k, n):
                    act.wait_ge(w_used, b.w_end)
                    act.drain()
                    for t in range(TT):
                        nc.scalar.activation(s[:, t, 0:n], pair[b.g % 2][:, t, 0:n], ACT.Square,
                                             accum_out=ssq[:, t, 0:1]).then_inc(sq_ready, 1)
                    root(k)

                for n in range(1, 8):
                    for u in range(8):
                        if u == 4:
                            if n == 1:
                                small_squares(win[0], N_QA, Q_RANK)
                            elif n == 2:
                                small_squares(win[1], N_KV, KV_RANK)
                            elif n <= 6:
                                act.drain()
                                if n > 3:
                                    act.wait_ge(t_full, tp["fqk"] + 2 * (n - 3))
                                stage(win[n - 1], lambda t: s[:, t, :])
                            else:
                                stage(win[6], lambda t: fv[:, t, 0:NB])
                        cols = KV_RANK + ROPE + HEADS if n == 1 else NB
                        hi_unit(win[n], u, n=cols)
                    if n == 1:
                        hi_mod(tp["qa"], qa_hi, 2)
                    if n == 2:
                        hi_mod(tp["kv"], ka_hi, 1)
                    if n == 3:
                        act.wait_ge(fz_v, 1)
                        nc.scalar.activation(fz[:, 3], fz[:, 2], ACT.Exp, scale=-1.0).then_inc(fz_a, 1)
                        act.wait_ge(fz_v, 2)
                        nc.scalar.activation(fz[:, 4], fz[:, 3], ACT.Ln).then_inc(fz_a, 1)
                uq, ukv, wo = pl["uq"], pl["ukv"], pl["wo"]
                to_q = lambda b: (lambda t: y[:, t, b * NB:(b + 1) * NB])
                to_kv = lambda b: (lambda t: kv[:, t, b * NB:(b + 1) * NB])
                hi_unit(uq[0], 0)
                hi_unit(uq[0], 1)
                hi_unit(uq[1], 0)
                hi_unit(uq[1], 1)
                stage(win[7], lambda t: fv[:, t, NB:2 * NB])
                hi_unit(uq[2], 0)
                hi_unit(uq[2], 1)
                stage(uq[0], to_q(0))
                hi_unit(ukv[0], 0)
                hi_unit(ukv[1], 0)
                stage(uq[1], to_q(1))
                hi_unit(ukv[2], 0)
                hi_unit(ukv[3], 0)
                stage(uq[2], to_q(2))
                for b in range(4):
                    hi_unit(wo[0], b)
                    stage(ukv[b], to_kv(b))
                for k in range(4):
                    act.wait_ge(t_full, tp["qn"] + k + 1)
                    nc.scalar.activation(qnT[:, 2 * k:2 * k + 2, :],
                                         tps[:, (tp["qn"] + k) % 2, :].rearrange("p (c t) -> p c t", c=2),
                                         ACT.Copy).then_inc(t_taken["a"], 1)
                o_hi = lambda n: (n + HEADS) % N_ATT
                for n in range(N_ATT + 3):
                    if n >= 3:
                        m = n - 3
                        act.wait_ge(o_full, m + 1)
                        nc.scalar.activation(h_hi[:, o_hi(m), :], mps[:, m % 2, 0:SEQ], ACT.Copy).then_inc(ohi_ready, 1)
                    if n < N_ATT:
                        scale = FOX_SCALE if n < HEADS else MLA_SCALE
                        sb_n = pair[(n % 4) // 2][:, n % 2, :]
                        act.wait_ge(nbias_ready, n + 1)
                        if n >= 2:
                            act.wait_ge(t_full, tp["pt"] + n - 1)
                        for t in range(TT):
                            k0, k1 = (0, P) if t == 0 else (P, 3 * P)
                            ins = nc.scalar.activation(prob[:, n % 2, k0:k1], sb_n[:, k0:k1], ACT.Exp,
                                                       bias=nbias[:, n % 2, t:t + 1], scale=scale,
                                                       accum_out=rsum[:, n % 2, t:t + 1])
                        ins.then_inc(exp_ready, 1)
                    if 2 <= n < N_ATT + 2:
                        m = n - 2
                        act.wait_ge(t_full, tp["pt"] + m + 1)
                        if m >= 2:
                            act.wait_ge(o_full, m - 1)
                        nc.scalar.activation(probT[:, m % 2, :], tps[:, (tp["pt"] + m) % 2, 0:3 * P],
                                             ACT.Copy).then_inc(t_taken["a"], 1)
                gate_row(gate_mix, tp["gatemix"], 0, 4)
                for n, b in enumerate(wo):
                    for u in range(8):
                        if n == 0 and u < 4:
                            continue
                        if u == 4 and n:
                            square_y(wo[n - 1], N_YM, n - 1)
                        hi_unit(b, u)
                square_y(wo[-1], N_YM, DB - 1)
                root(N_YM)

        @block.vector
        def _(dve):
            def lo_unit(b, u, i=0, per=0, per_w=0, n=NB):
                r, w = b.r_of(u), b.w + u
                dve.wait_ge(hi_ready, plus(w + 1, i, per_w))
                nc.vector.tensor_tensor(w_lo[:, w % RING, :, 0:n], raw[:, r % RING, :, 0:n],
                                        w_hi[:, w % RING, :, 0:n], ALU.subtract).then_inc(raw_used, 1)

            def ada_unit(b, n, a, i=0, per=0):
                r, q = b.r + n, a // 8
                if a % 8:
                    dve.drain()
                dve.wait_ge(raw_landed[r % RING], landed(r, i, per))
                for k in range(2):
                    j = 2 * (a % 8) + k
                    if j == 0:
                        ins = nc.vector.tensor_scalar(acc[:, q, :], raw[:, r % RING, 0, :], c_col[:, 1, 0:1],
                                                      None, ALU.mult)
                        continue
                    if k:
                        dve.drain()
                    ins = nc.vector.scalar_tensor_tensor(acc[:, q, :], raw[:, r % RING, k, :], c_col[:, 1, j:j + 1],
                                                         acc[:, q, :], ALU.mult, ALU.add)
                ins.then_inc(raw_used, 1)

            def run(b, tasks=None, i=0, per=0, per_w=0, start=0, stop=None, n=NB):
                a = b.seq.index(("W", start)) if start else 0
                z = b.seq.index(("W", stop)) if stop else len(b.seq)
                for at in range(a, z):
                    kind, u = b.seq[at]
                    if kind == "A":
                        ada_unit(b, at, u, i, per)
                        continue
                    if tasks and u in tasks:
                        tasks[u]()
                    lo_unit(b, u, i, per, per_w, n)

            def mod_columns(b, i=0, per_q=0):
                k, c0 = DB * b.na // 8, plus(DB * b.q, i, DB * per_q)
                dve.wait_ge(sum_ready, plus(b.m + 1, i, int(per_q > 0)))
                nc.vector.tensor_tensor(mod[:, bass.ds(c0, k)], mps[:, 0, 0:k], col[:, bass.ds(c0, k)],
                                        ALU.add).then_inc(mod_ready, 1)

            def power(k, n_sq, width, columns):
                dve.wait_ge(sq_ready, SQ[k] + n_sq)
                if columns > 1:
                    nc.vector.tensor_reduce(ms[:], ssq[:], AX_X, ALU.add)
                    dve.drain()
                    nc.vector.tensor_scalar(ms[:], ms[:], 1.0 / width, EPS, ALU.mult, ALU.add)
                else:
                    nc.vector.tensor_scalar(ms[:], ssq[:, :, 0], 1.0 / width, EPS, ALU.mult, ALU.add)
                dve.drain()
                nc.vector.reciprocal(inv_ms[:], ms[:]).then_inc(ms_ready, 1)

            def refine(k):
                dve.wait_ge(rstd_ready, k + 1)
                nc.vector.scalar_tensor_tensor(newton[:], rstd[:], -0.5, rstd[:], ALU.mult, ALU.mult)
                dve.drain()
                nc.vector.tensor_tensor(newton[:], newton[:], ms[:], ALU.mult)
                dve.drain()
                nc.vector.scalar_tensor_tensor(rstd[:], newton[:], 1.5, rstd[:], ALU.add, ALU.mult)
                dve.drain()

            def update_x(k):
                refine(k)
                for t in range(TT):
                    for b in range(DB):
                        c = slice(b * NB, (b + 1) * NB)
                        nc.vector.scalar_tensor_tensor(x[:, t, c], y[:, t, c], rstd[:, t:t + 1], x[:, t, c],
                                                       ALU.mult, ALU.add).then_inc(x_ready, 1)

            def normalise_x(k):
                refine(k)
                for h in range(2):
                    for t in range(TT):
                        c = slice(h * D // 2, (h + 1) * D // 2)
                        nc.vector.tensor_scalar(y[:, t, c], x[:, t, c], rstd[:, t:t + 1], None,
                                                ALU.mult).then_inc(xn_ready, 1)

            def modulate(name, th, dst_hi, dst_lo, gain, shift, n_pieces, between=None):
                t0 = tp[name]

                def lo(cp):
                    dve.wait_ge(t_hi, TH[th] + cp + 1)
                    nc.vector.tensor_tensor(dst_lo[:, 2 * cp:2 * cp + 2, :],
                                            tmp[:, cp % 2, :].rearrange("p (c t) -> p c t", c=2),
                                            dst_hi[:, 2 * cp:2 * cp + 2, :], ALU.subtract).then_inc(h_ready, 1)

                for cp in range(n_pieces):
                    if between is not None and cp in (2, 4, 6):
                        between(cp // 2 + 1)
                    dve.wait_ge(t_full, t0 + cp + 1)
                    if cp == 0 or cp >= 2:
                        dve.drain()
                    for c in range(2):
                        k = 2 * cp + c
                        half = slice(c * SEQ, (c + 1) * SEQ)
                        if shift is None:
                            ins = nc.vector.tensor_scalar(tmp[:, cp % 2, half], tps[:, (t0 + cp) % 2, half],
                                                          gain[:, k:k + 1], None, ALU.mult)
                        else:
                            ins = nc.vector.tensor_scalar(tmp[:, cp % 2, half], tps[:, (t0 + cp) % 2, half],
                                                          gain[:, k:k + 1], shift[:, k:k + 1], ALU.mult, ALU.add)
                    ins.then_inc(t_taken["v"], 1)
                    if cp:
                        lo(cp - 1)
                lo(n_pieces - 1)

            def gain_columns(v, pre):
                nc.vector.scalar_tensor_tensor(a_col[:], mod[:, (v + 1) * KD:(v + 2) * KD], 1.0,
                                               col[:, pre:pre + KD], ALU.add, ALU.mult)
                dve.drain()
                return mod[:, v * KD:(v + 1) * KD]

            def gate_columns(v, post, weight):
                nc.vector.scalar_tensor_tensor(g_col[:], mod[:, v * KD:(v + 1) * KD], weight,
                                               col[:, post:post + KD], ALU.mult, ALU.mult)
                dve.drain()

            def diagonals(j, t0, first=False):
                if not first:
                    dve.wait_ge(t_full, t0 + 1)
                for k in range(4):
                    ins = nc.vector.tensor_scalar(tmp[:, j % 2, k * P:(k + 1) * P], ident,
                                                  g_col[:, 4 * j + k:4 * j + k + 1], None, ALU.mult)
                ins.then_inc(dg_ready, 1)

            def hidden(b, i=0, per_w=0, per_g=0):
                g = b.g + 1
                dve.wait_ge(evac[b.g % 2], plus(b.g // 2 + 1, i, per_g))
                dve.wait_ge(w_used, plus(b.w + 16, i, per_w))
                for t in range(TT):
                    ins = nc.vector.tensor_tensor(s[:, t, :], s[:, t, :], pair[g % 2][:, t, :], ALU.mult)
                ins.then_inc(evac[g % 2], 1)

            def lo_hid(t0, th0, c0, i=0, per_t=0):
                for k in range(2):
                    dve.wait_ge(t_hi, plus(th0 + k + 1, i, per_t))
                    nc.vector.tensor_tensor(hid_lo[:, bass.ds(c0 + 2 * k, 2), :],
                                            tps[:, (t0 + k) % 2, :].rearrange("p (c t) -> p c t", c=2),
                                            hid_hi[:, bass.ds(c0 + 2 * k, 2), :],
                                            ALU.subtract).then_inc(t_taken["v"], 1)

            def evac_y(b, k, blk, gate, gate_fill):
                dve.wait_ge(sq_ready, SQ[k] + 2 * (blk + 1))
                dve.wait_ge(t_taken["a"], taken[gate_fill][1])
                c = slice(blk * NB, (blk + 1) * NB)
                for t in range(TT):
                    ins = nc.vector.tensor_tensor(y[:, t, c], pair[b.g % 2][:, t, :], gate[:, c], ALU.mult)
                ins.then_inc(evac[b.g % 2], 1)

            dve.wait_ge(small_landed, SMALL)
            nc.vector.tensor_copy(msk[:, 0, :], ident)
            nc.vector.tensor_copy(msk[:, 1:3, :], cst[:, C_MF:C_MF + 2 * P].rearrange("p (m q) -> p m q", m=2))
            dve.wait_ge(cols_full, 1)
            nc.vector.tensor_copy(col[:], mps[:, 1, 0:V_ROWS]).then_inc(setup, 1)
            dve.wait_ge(setup, 1)
            dve.wait_ge(c_ready, 1)
            pre = pl["pre"]
            run(pre[0])
            mod_columns(pre[0])
            power(N_X0, 8, D, DB)
            normalise_x(N_X0)
            with dve.Fori(0, 3) as i:
                run(pre[1], None, i, 16)
                mod_columns(pre[1], i, 2)

            for f, gu, down in (("1", "gu1", "down1"), ("2", "gu2", "down2")):
                first, second = pl[gu][0], pl[gu][1]
                per, t0, th = len(second.seq), tp["hid" + f], TH["hid" + f]
                pre_v = 0 if f == "1" else 6
                lo_unit(first, 0)
                if f == "2":
                    update_x(N_YM)
                    lo_unit(first, 1)
                    mod_columns(pl["wo"][-1])
                    power(N_XM, 8, D, DB)
                    normalise_x(N_XM)
                else:
                    lo_unit(first, 1)
                dve.drain()
                shift = gain_columns(pre_v, G_PRE["ffn" + f])
                modulate("mod" + f, "mod" + f, h_hi, h_lo, a_col, shift, 8, lambda u: run(first, start=u, stop=u + 1))
                run(first, start=5)
                with dve.Fori(0, FB - 1) as i:
                    def last_block():
                        hidden(first, i, 16, 1)
                        if first.na and f == "1":
                            mod_columns(first, i, 1)
                    run(second, {4: last_block, 7: lambda: lo_hid(t0, th, i * 4, i, 2)}, i, per, 16)
                b0, last = pl[down][0], pl[gu][-1]
                if f == "2":
                    mod_columns(first)
                dve.drain()
                gate_columns(pre_v + 2, G_POST["ffn" + f], 0.5)
                diagonals(0, 0, True)
                diagonals(1, 0, True)
                lo_unit(b0, 0)
                lo_unit(b0, 1)
                hidden(last)
                if f == "1":
                    mod_columns(last)
                lo_hid(tp["hidlast" + f], th + 2 * (FB - 1), 4 * (FB - 1))
                diagonals(2, tp["gate" + f])
                diagonals(3, tp["gate" + f] + 1)
                k_y = N_Y1 if f == "1" else N_Y2
                fills = [tp["gate" + f], tp["gate" + f] + 1, tp["gateb" + f], tp["gateb" + f] + 1]
                for n, b in enumerate(pl[down]):
                    def last_down(n=n):
                        if n:
                            evac_y(pl[down][n - 1], k_y, n - 1, gate_ffn, fills[n - 1])
                            if pl[down][n - 1].na:
                                mod_columns(pl[down][n - 1])
                    run(b, {4: last_down}, start=2 if n == 0 else 0)
                evac_y(pl[down][-1], k_y, DB - 1, gate_ffn, fills[-1])
                power(k_y, 8, D, DB)
                if f == "2":
                    update_x(k_y)
                    break

                win = pl["win"]
                lo_unit(win[0], 0)
                update_x(N_Y1)
                lo_unit(win[0], 1)
                mod_columns(pl["down1"][-1])
                power(N_X1, 8, D, DB)
                normalise_x(N_X1)
                shift = gain_columns(3, G_PRE["mix"])
                modulate("modmix", "modmix", h_hi, h_lo, a_col, shift, 8, lambda u: run(win[0], start=u, stop=u + 1))
                run(win[0], start=5)

                def take_qa():
                    b = win[0]
                    power(N_QA, 2, Q_RANK, 1)
                    refine(N_QA)
                    for t in range(TT):
                        ins = nc.vector.tensor_scalar(y[:, t, 0:Q_RANK], pair[b.g % 2][:, t, :], rstd[:, t:t + 1],
                                                      None, ALU.mult)
                    ins.then_inc(evac[b.g % 2], 1)

                def take_kv():
                    b = win[1]
                    bank = pair[b.g % 2]
                    power(N_KV, 2, KV_RANK, 1)
                    nc.vector.tensor_copy(kpe[:, 0], bank[:, :, KV_RANK:KV_RANK + ROPE])
                    nc.vector.tensor_tensor(fz[:, 1], bank[:, :, KV_RANK + ROPE:KV_RANK + ROPE + HEADS],
                                            fz[:, 0, 0:1, :].to_broadcast([P, TT, HEADS]), ALU.add)
                    refine(N_KV)
                    for t in range(TT):
                        ins = nc.vector.tensor_scalar(y[:, t, Q_RANK:Q_RANK + KV_RANK], bank[:, t, 0:KV_RANK],
                                                      rstd[:, t:t + 1], None, ALU.mult)
                    ins.then_inc(evac[b.g % 2], 1)
                    dve.drain()
                    nc.vector.scalar_tensor_tensor(fz[:, 2], fz[:, 1], -1.0, fz[:, 1], ALU.mult,
                                                   ALU.max).then_inc(fz_v, 1)

                def rotate(x1, x2, o1, o2, cos, sin, shape):
                    dve.drain()
                    size = shape[1] * shape[2]
                    part = [tmp[:, k // 2, (k % 2) * size:(k % 2 + 1) * size].rearrange("p (a b) -> p a b", a=shape[1])
                            for k in range(4)]
                    for k, (u, v) in enumerate(((x1, cos), (x2, sin), (x1, sin), (x2, cos))):
                        nc.vector.tensor_tensor(part[k], u, v, ALU.mult)
                    dve.drain()
                    nc.vector.tensor_tensor(o1, part[0], part[1], ALU.subtract)
                    return nc.vector.tensor_tensor(o2, part[2], part[3], ALU.add)

                half = ROPE // 2
                cos = cst[:, C_COS:C_COS + TT * half].rearrange("p (t e) -> p t e", t=TT)
                sin = cst[:, C_SIN:C_SIN + TT * half].rearrange("p (t e) -> p t e", t=TT)

                def copy_fill(n, dst, rows=P, width=2):
                    dve.wait_ge(t_full, n + 1)
                    src = tps[0:rows, n % 2, 0:width * SEQ]
                    if width > 1:
                        src = src.rearrange("p (c t) -> p c t", c=width)
                    nc.vector.tensor_copy(dst, src).then_inc(t_taken["v"], 1)

                for n in range(1, 8):
                    tasks = {}
                    if win[n - 1].na:
                        tasks[3] = lambda n=n: mod_columns(win[n - 1])
                    if n == 1:
                        tasks[4] = take_qa
                    if n == 2:
                        tasks[4] = take_kv
                    run(win[n], tasks, n=KV_RANK + ROPE + HEADS if n == 1 else NB)
                    if n == 1:
                        modulate("qa", "qa", qa_hi, qa_lo, col[:, G_QA:G_QA + 4], None, 2)
                    if n == 2:
                        modulate("kv", "kv", ka_hi, ka_lo, col[:, G_KV:G_KV + 2], None, 1)
                        rotate(kpe[:, 0, :, 0:half], kpe[:, 0, :, half:], kpe[:, 1, :, 0:half], kpe[:, 1, :, half:],
                               cos, sin, [P, TT, half]).then_inc(rot_ready, 1)
                    if n == 3:
                        nc.vector.memset(krT[ROPE:P, :], 0.0)
                        nc.vector.memset(qrT[ROPE:P, :, :], 0.0)
                        nc.vector.memset(cumT[:], 0.0)
                        copy_fill(tp["kpe"], krT[0:ROPE, :], ROPE, 1)
                        dve.wait_ge(fz_a, 1)
                        nc.vector.tensor_scalar(fz[:, 3], fz[:, 3], 1.0, None, ALU.add).then_inc(fz_v, 1)
                    if n == 4:
                        dve.wait_ge(fz_a, 2)
                        nc.vector.scalar_tensor_tensor(fz[:, 4], fz[:, 1], 0.0, fz[:, 4], ALU.min,
                                                       ALU.subtract).then_inc(fz_v, 1)
                    if n == 5:
                        dve.wait_ge(cum_full, 1)
                        nc.vector.tensor_copy(cumT[0:HEADS, :], mps[0:HEADS, 1, 0:SEQ]).then_inc(cum_ready, 1)
                    if 3 <= n <= 6:
                        for k in range(2):
                            h = 4 * (n - 3) + 2 * k
                            copy_fill(tp["fqk"] + 2 * (n - 3) + k, fqk[:, h:h + 2, :])
                uq, ukv, wo = pl["uq"], pl["ukv"], pl["wo"]
                lo_unit(uq[0], 0)
                mod_columns(win[7])
                lo_unit(uq[0], 1)
                for b in uq[1:]:
                    lo_unit(b, 0)
                    lo_unit(b, 1)
                for b in ukv:
                    lo_unit(b, 0)
                dve.wait_ge(evac[uq[2].g % 2], uq[2].g // 2 + 1)
                for t in range(TT):
                    q = y[:, t, 0:HEADS * QK].rearrange("p (h e) -> p h e", h=HEADS)
                    q1, q2 = q[:, :, NOPE:NOPE + half], q[:, :, NOPE + half:QK]
                    c, d = (v[:, t:t + 1, :].to_broadcast([P, HEADS, half]) for v in (cos, sin))
                    rotate(q1, q2, q1, q2, c, d, [P, HEADS, half]).then_inc(rot_ready, 1)
                run(wo[0], stop=4)
                for k in range(4):
                    copy_fill(tp["kn"] + k, knT[:, 2 * k:2 * k + 2, :])
                for k in range(4):
                    copy_fill(tp["qr"] + k, qrT[0:ROPE, 2 * k:2 * k + 2, :], ROPE)

                for n in range(N_ATT + 3):
                    if n < N_ATT:
                        bank = pair[(n % 4) // 2][:, n % 2, :]
                        dve.wait_ge(score_full, n + 1)
                        if n >= 2:
                            dve.wait_ge(exp_ready, n - 1)
                        for t in range(TT):
                            k0, k1 = (0, P) if t == 0 else (P, 3 * P)
                            nc.vector.tensor_reduce(nmax[:, n % 2, t:t + 1], bank[:, k0:k1], AX_X, ALU.max)
                        dve.drain()
                        nc.vector.tensor_scalar(nbias[:, n % 2, :], nmax[:, n % 2, :],
                                                -(FOX_SCALE if n < HEADS else MLA_SCALE), None,
                                                ALU.mult).then_inc(nbias_ready, 1)
                    if 1 <= n < N_ATT + 1:
                        m = n - 1
                        dve.wait_ge(exp_ready, m + 1)
                        nc.vector.reciprocal(rinv[:, m % 2, :], rsum[:, m % 2, :])
                        dve.drain()
                        for t in range(TT):
                            k0, k1 = (0, P) if t == 0 else (P, 3 * P)
                            ins = nc.vector.tensor_scalar(prob[:, m % 2, k0:k1], prob[:, m % 2, k0:k1],
                                                          rinv[:, m % 2, t:t + 1], None, ALU.mult)
                        ins.then_inc(prob_ready, 1)
                    if n == N_ATT:
                        gate_columns(5, G_POST["mix"], 1.0)
                        diagonals(0, 0, True)
                        diagonals(1, 0, True)
                    if n >= 3:
                        m = n - 3
                        o = (m + HEADS) % N_ATT
                        dve.wait_ge(ohi_ready, m + 1)
                        nc.vector.tensor_tensor(h_lo[:, o, :], mps[:, m % 2, 0:SEQ], h_hi[:, o, :],
                                                ALU.subtract).then_inc(o_ready, 1)
                diagonals(2, tp["gatemix"])
                diagonals(3, tp["gatemix"] + 1)
                for n, b in enumerate(wo):
                    tasks = {}
                    if n:
                        tasks[3] = lambda n=n: mod_columns(wo[n - 1])
                        tasks[4] = lambda n=n: evac_y(wo[n - 1], N_YM, n - 1, gate_mix, tp["gatemix"] + n - 1)
                    run(b, tasks, start=4 if n == 0 else 0)
                evac_y(wo[-1], N_YM, DB - 1, gate_mix, tp["gatemix"] + DB - 1)
                power(N_YM, 8, D, DB)

        @block.tensor
        def _(pe):
            def unit(b, u, lhs_hi, lhs_lo, k0, g, first, last, i=0, per=0, per_w=0, n=NB):
                r, w = b.r_of(u), b.w + u
                pe.wait_ge(raw_used, plus(r + 1, i, per))
                for kk in range(2):
                    for t in range(TT):
                        o = pair[g % 2][:, t, 0:n]
                        hi = lhs_hi[:, k0 + kk, t * P:(t + 1) * P]
                        lo = lhs_lo[:, k0 + kk, t * P:(t + 1) * P]
                        wh, wl = w_hi[:, w % RING, kk, 0:n], w_lo[:, w % RING, kk, 0:n]
                        nc.tensor.matmul(o, hi, wh, start=first and kk == 0, stop=False)
                        nc.tensor.matmul(o, hi, wl, start=False, stop=False)
                        ins = nc.tensor.matmul(o, lo, wh, start=False, stop=last and kk == 1)
                ins.then_inc(w_used, 1)

            def bank_free(g, i=0, per_g=0):
                if per_g or g >= 2:
                    pe.wait_ge(evac[g % 2], plus(g // 2, i, per_g))

            def fill_free(n, i=0, per_t=0):
                if n >= 2:
                    who, count = taken[n - 2]
                    pe.wait_ge(t_taken[who], plus(count, i, per_t))

            def transposes(n, parts, i=0, per_t=0):
                fill_free(n, i, per_t)
                for k, src in enumerate(parts):
                    rows = src.shape[1]
                    ins = nc.tensor.transpose(tps[0:rows, n % 2, k * P:(k + 1) * P], src, ident)
                ins.then_inc(t_full, 1)

            def turn_x(n, k):
                for cp in range(8):
                    if cp % 4 == 0:
                        pe.wait_ge(xn_ready, k + 2 + 2 * (cp // 4))
                    transposes(n + cp, [y[:, t, c * P:(c + 1) * P] for c in (2 * cp, 2 * cp + 1) for t in range(TT)])

            def turn_s(n, i=0, per_t=0):
                for k in range(2):
                    transposes(n + k, [s[:, t, c * P:(c + 1) * P] for c in (2 * k, 2 * k + 1) for t in range(TT)],
                               i, per_t)

            def sum_columns(b, i=0, per=0, per_m=0):
                last_a = b.r + max(n for n, (kind, _) in enumerate(b.seq) if kind == "A")
                pe.wait_ge(raw_used, plus(last_a + 1, i, per))
                if per_m or b.m:
                    pe.wait_ge(mod_ready, plus(b.m, i, per_m))
                for k in range(DB * b.na // 8):
                    ins = nc.tensor.matmul(mps[:, 0, k:k + 1], acc[:, k // 4, (k % 4) * P:(k % 4 + 1) * P],
                                           ones[:, 0:1], start=True, stop=True)
                ins.then_inc(sum_ready, 1)

            def gate_rows(t0, dg0, n):
                for j in range(n):
                    pe.wait_ge(dg_ready, dg0 + j + 1)
                    fill_free(t0 + j)
                    nc.tensor.matmul(tps[:, (t0 + j) % 2, :], ones, tmp[:, (dg0 + j) % 2, :],
                                     start=True, stop=True).then_inc(t_full, 1)

            def gate_up(b, i=0, per=0, per_w=0, per_g=0, ready=None, after=None):
                for u in range(16):
                    g = b.g + u // 8
                    if u % 8 == 0:
                        bank_free(g, i, per_g)
                    if ready is not None and u < 8:
                        pe.wait_ge(h_ready, ready + u + 1)
                    unit(b, u, h_hi, h_lo, 2 * (u % 8), g, u % 8 == 0, u % 8 == 7, i, per, per_w)
                    if after is not None and u == 2:
                        after()

            pe.wait_ge(small_landed, SMALL)
            nc.tensor.transpose(mps[:, 1, 0:P], y[:, 0, 0:P], ident)
            rest = V_ROWS - P
            nc.tensor.transpose(mps[:, 1, P:V_ROWS], y[0:rest, 0, P:2 * P], cst[0:rest, 0:rest]).then_inc(cols_full, 1)
            pre = pl["pre"]
            sum_columns(pre[0])
            with pe.Fori(0, 3) as i:
                sum_columns(pre[1], i, 16, 1)

            for f, gu, down in (("1", "gu1", "down1"), ("2", "gu2", "down2")):
                first, second = pl[gu][0], pl[gu][1]
                per, t0 = len(second.seq), tp["hid" + f]
                turn_x(tp["mod" + f], XN["ffn" + f])
                gate_up(first, ready=HR["ffn" + f])
                if first.na:
                    sum_columns(first)
                with pe.Fori(0, FB - 1) as i:
                    def turn_last():
                        pe.wait_ge(evac[(first.g + 1) % 2], (first.g + 1) // 2 + 1 + i)
                        turn_s(t0, i, 2)
                    gate_up(second, i, per, 16, 1, after=turn_last)
                    if second.na:
                        sum_columns(second, i, per, 1)
                last = pl[gu][-1]
                dg0 = DG["ffn" + f]
                gate_rows(tp["gate" + f], dg0, 2)
                pe.wait_ge(evac[(last.g + 1) % 2], (last.g + 1) // 2 + 1)
                turn_s(tp["hidlast" + f])
                gate_rows(tp["gateb" + f], dg0 + 2, 2)
                who, count = taken[tp["hidlast" + f] + 1]
                pe.wait_ge(t_taken[who], count)
                b0, b1 = pl[down][0], pl[down][1]
                with pe.Fori(0, 2) as i:
                    for b in (b0, b1):
                        bank_free(b.g, i, 1)
                        for u in range(22):
                            unit(b, u, hid_hi, hid_lo, 2 * u, b.g, u == 0, u == 21, i, 2 * len(b.seq), 44)
                        if b.na:
                            sum_columns(b, i, 2 * len(b.seq), 2)
                if f == "2":
                    break

                win = pl["win"]
                turn_x(tp["modmix"], XN["mix"])
                for n, b in enumerate(win):
                    bank_free(b.g)
                    for u in range(8):
                        if n == 0:
                            pe.wait_ge(h_ready, HR["mix"] + u + 1)
                        unit(b, u, h_hi, h_lo, 2 * u, b.g, u == 0, u == 7,
                             n=KV_RANK + ROPE + HEADS if n == 1 else NB)
                        if u == 5 and n:
                            prev = win[n - 1]
                            if n <= 6:
                                pe.wait_ge(evac[prev.g % 2], prev.g // 2 + 1)
                            if n == 1:
                                for k in range(2):
                                    transposes(tp["qa"] + k, [y[:, t, c * P:(c + 1) * P]
                                                              for c in (2 * k, 2 * k + 1) for t in range(TT)])
                            if n == 2:
                                transposes(tp["kv"], [y[:, t, Q_RANK + c * P:Q_RANK + (c + 1) * P]
                                                      for c in range(2) for t in range(TT)])
                            if n == 3:
                                pe.wait_ge(rot_ready, 1)
                                transposes(tp["kpe"], [kpe[:, 1, t, :] for t in range(TT)])
                            if 3 <= n <= 6:
                                turn_s(tp["fqk"] + 2 * (n - 3))
                            if n == 5:
                                pe.wait_ge(fz_v, 3)
                                lf = [fz[:, 4, t, :] for t in range(TT)]
                                nc.tensor.matmul(mps[0:HEADS, 1, 0:P], lf[0], tri, start=True, stop=True)
                                nc.tensor.matmul(mps[0:HEADS, 1, P:SEQ], lf[0], ones, start=True, stop=False)
                                nc.tensor.matmul(mps[0:HEADS, 1, P:SEQ], lf[1], tri, start=False,
                                                 stop=True).then_inc(cum_full, 1)
                    if b.na:
                        sum_columns(b)
                uq, ukv, wo = pl["uq"], pl["ukv"], pl["wo"]
                pe.wait_ge(h_ready, HR["kv"] + 1)
                for b in uq:
                    bank_free(b.g)
                    for u in range(2):
                        unit(b, u, qa_hi, qa_lo, 2 * u, b.g, u == 0, u == 1)
                for b in ukv:
                    bank_free(b.g)
                    unit(b, 0, ka_hi, ka_lo, 0, b.g, True, True)
                for k in range(4):
                    hs = (2 * k, 2 * k + 1)
                    transposes(tp["qn"] + k, [y[:, t, h * QK:h * QK + NOPE] for h in hs for t in range(TT)])
                for b in ukv[2:]:
                    pe.wait_ge(evac[b.g % 2], b.g // 2 + 1)
                for k in range(4):
                    hs = (2 * k, 2 * k + 1)
                    transposes(tp["kn"] + k, [kv[:, t, h * 2 * P:h * 2 * P + NOPE] for h in hs for t in range(TT)])
                pe.wait_ge(rot_ready, 1 + TT)
                for k in range(4):
                    hs = (2 * k, 2 * k + 1)
                    transposes(tp["qr"] + k, [y[:, t, h * QK + NOPE:(h + 1) * QK] for h in hs for t in range(TT)])

                pe.wait_ge(sel_landed, 16)
                pe.wait_ge(cum_ready, 1)
                pe.wait_ge(mod_ready, pl["win"][-1].m + 1)

                def scores(n):
                    bank = pair[(n % 4) // 2][:, n % 2, :]
                    if n >= 4:
                        pe.wait_ge(exp_ready, n - 3)
                    for t in range(TT):
                        q = slice(t * P, (t + 1) * P)
                        keys = slice(0, (t + 1) * P)
                        o = bank[:, P * t:P * t + (t + 1) * P]
                        diagonal = bank[:, P * t + t * P:P * t + (t + 1) * P]
                        if n < HEADS:
                            nc.tensor.matmul(o, fqk[:, n, q], fqk[:, HEADS + n, keys], start=True, stop=False)
                            nc.tensor.matmul(diagonal, msk[:, 0, :], msk[:, 1, :], start=False, stop=False)
                            ins = nc.tensor.matmul(o, sel[:, n, :], cumT[:, keys], start=False, stop=True)
                        else:
                            h = n - HEADS
                            nc.tensor.matmul(o, qnT[:, h, q], knT[:, h, keys], start=True, stop=False)
                            nc.tensor.matmul(diagonal, msk[:, 0, :], msk[:, 2, :], start=False, stop=False)
                            ins = nc.tensor.matmul(o, qrT[:, h, q], krT[:, keys], start=False, stop=True)
                    ins.then_inc(score_full, 1)

                def outputs(m):
                    pe.wait_ge(t_taken["a"], taken[tp["pt"] + m][1])
                    if m >= 2:
                        pe.wait_ge(o_ready, m - 1)
                    h = m % HEADS
                    if m < HEADS:
                        v = [fv[:, t, h * P:(h + 1) * P] for t in range(TT)]
                    else:
                        v = [kv[:, t, h * 2 * P + NOPE:(h + 1) * 2 * P] for t in range(TT)]
                    pt = probT[:, m % 2, :]
                    o = mps[:, m % 2, :]
                    nc.tensor.matmul(o[:, 0:P], v[0], pt[:, 0:P], start=True, stop=True)
                    nc.tensor.matmul(o[:, P:SEQ], v[0], pt[:, P:2 * P], start=True, stop=False)
                    nc.tensor.matmul(o[:, P:SEQ], v[1], pt[:, 2 * P:3 * P], start=False, stop=True).then_inc(o_full, 1)

                for n in range(N_ATT + 2):
                    if n < N_ATT:
                        if n == HEADS:
                            who, count = taken[tp["qr"] + 3]
                            pe.wait_ge(t_taken[who], count)
                        scores(n)
                    if 1 <= n < N_ATT + 1:
                        m = n - 1
                        pe.wait_ge(prob_ready, m + 1)
                        transposes(tp["pt"] + m, [prob[:, m % 2, k * P:(k + 1) * P] for k in range(3)])
                    if n >= 2:
                        outputs(n - 2)
                gate_rows(tp["gatemix"], DG["mix"], 4)
                pe.wait_ge(o_ready, N_ATT)
                b0, b1 = wo[0], wo[1]
                with pe.Fori(0, 2) as i:
                    for b in (b0, b1):
                        bank_free(b.g, i, 1)
                        for u in range(8):
                            unit(b, u, h_hi, h_lo, 2 * u, b.g, u == 0, u == 7, i, 2 * len(b.seq), 16)
                        sum_columns(b, i, 2 * len(b.seq), 2)


_NAMES = ["x", "c", "w_ada", "b_ada", "w1_gate", "w1_up", "w1_down", "w_in", "b_forget", "w_uq", "w_ukv", "w_o",
          "w2_gate", "w2_up", "w2_down"]


def constants():
    j = np.arange(P)
    cst = np.zeros((P, C_ALL), np.float32)
    cst[:, C_ID:C_ID + P] = np.eye(P)
    cst[:, C_TRI:C_TRI + P] = j[:, None] <= j[None, :]
    cst[:, C_ONE:C_ONE + P] = 1.0
    cst[:, C_MF:C_MF + P] = np.where(j[None, :] <= j[:, None], 0.0, MASKED)
    cst[:, C_MM:C_MM + P] = np.where(j[None, :] // CHUNK <= j[:, None] // CHUNK, 0.0, MASKED)
    half = ROPE // 2
    inv = np.float32(10000.0) ** (-np.arange(half, dtype=np.float32) / np.float32(half))
    ang = np.arange(SEQ, dtype=np.float32)[:, None] * inv[None, :].astype(np.float32)
    for at, f in ((C_COS, np.cos), (C_SIN, np.sin)):
        v = f(ang.astype(np.float32)).astype(np.float32).reshape(TT, P, half)
        cst[:, at:at + TT * half] = v.transpose(1, 0, 2).reshape(P, TT * half)
    sel = np.zeros((P, HEADS, P), np.float32)
    for h in range(HEADS):
        sel[h, h, :] = -1.0 / FOX_SCALE
    return cst, sel.reshape(P, HEADS * P)


def kernel(**inputs):
    import concourse.bacc as bacc
    from concourse.bass_utils import run_bass_kernel_spmd

    nc = bacc.Bacc("TRN2", target_bir_lowering=False, num_devices=1, dynamic_dma_scratch_size=1024)
    arrays = {}

    def given(name, a):
        a = np.ascontiguousarray(a)
        arrays[f"in_{name}"] = a
        return nc.dram_tensor(f"in_{name}", a.shape, F32, kind="ExternalInput").ap()

    A = {}
    for name in _NAMES:
        a = np.asarray(inputs[name])
        A[name] = given(name, a if name == "c" else a.reshape(a.shape[1:]))
    rows = lambda names: np.concatenate([np.asarray(inputs[n]).reshape(-1, P) for n in names])
    cst, sel = constants()
    const = {
        "gains": given("gains", rows(["g_ffn1_pre", "g_ffn1_post", "g_mix_pre", "g_mix_post", "g_ffn2_pre", "g_ffn2_post"])),
        "gains_a": given("gains_a", rows(["g_q_a", "g_kv_a"])),
        "cst": given("cst", cst),
        "sel": given("sel", sel),
    }
    out = nc.dram_tensor("out", (SEQ, D), F32, kind="ExternalOutput").ap()
    build(nc, A, const, out)
    r = run_bass_kernel_spmd(nc, [arrays], core_ids=[0])
    return r.results[0]["out"].reshape(1, SEQ, D)
```

```python
from contextlib import ExitStack

import numpy as np

import concourse.bass as bass
from concourse import mybir

F32 = mybir.dt.float32
F32R = mybir.dt.float32r
BF16 = mybir.dt.bfloat16
ALU = mybir.AluOpType
ACT = mybir.ActivationFunctionType
AX_X = mybir.AxisListType.X

P = 128
SEQ = 256
TT = SEQ // P
D = 2048
KD = D // P
FF = 5632
Q_RANK, KV_RANK = 512, 256
NOPE, ROPE, DV = 128, 64, 128
HEADS = 8
CHUNK = 64
EPS = 1e-6
N_MOD = 9
IN_WIDTH = Q_RANK + KV_RANK + ROPE + 3 * HEADS * P + HEADS
NB = 512
FB = FF // NB
DB = D // NB
QK = NOPE + ROPE
MLA_SCALE = float(QK) ** -0.5
FOX_SCALE = float(P) ** -0.5
MASKED = -1e38

C_ID, C_TRI, C_ONE, C_MF, C_MM = 0, P, 2 * P, 3 * P, 4 * P
C_COS, C_SIN = 5 * P, 5 * P + TT * ROPE // 2
C_ALL = 5 * P + TT * ROPE
G_PRE = {"ffn1": 144, "mix": 176, "ffn2": 208}
G_POST = {"ffn1": 160, "mix": 192, "ffn2": 224}
G_QA, G_KV = 240, 244
V_ROWS = 246

RING = 4


def pattern(n_w, ada_after):
    seq = []
    for u in range(n_w):
        seq.append(("W", u))
        for _ in range(ada_after.count(u)):
            seq.append(("A", sum(k == "A" for k, _ in seq)))
    return seq


class Block:

    def __init__(self, at, seq, products, quarter):
        self.r, self.w, self.g, self.m = at["r"], at["w"], at["g"], at["m"]
        self.seq = seq
        self.nw = sum(k == "W" for k, _ in seq)
        self.na = len(seq) - self.nw
        self.q = at["q"] if self.na else None
        assert self.na == 8 * quarter
        at["r"] += len(seq)
        at["w"] += self.nw
        at["g"] += products
        at["m"] += bool(self.na)
        at["q"] += quarter
        self.w_end = at["w"]

    def r_of(self, u):
        return self.r + self.seq.index(("W", u))


def make_plan():
    at = dict(r=0, w=0, g=0, m=0, q=0)
    pl = {}
    pl["pre"] = [Block(at, pattern_ada(16), 0, 2) for _ in range(4)]
    gu_ada = pattern(16, [4, 5, 7, 8, 10, 11, 13, 14])
    gu = pattern(16, [])
    gu_ada0 = pattern(16, list(range(8, 16)))
    pl["gu1"] = [Block(at, gu_ada if b else gu_ada0, 2, 1) for b in range(FB)]
    pl["down1"] = [Block(at, pattern(22, list(range(5, 21))), 1, 2) for _ in range(DB)]
    win_ada = pattern(8, [3, 4, 4, 5, 5, 6, 6, 7])
    pl["win"] = [Block(at, win_ada if b in (1, 5, 6, 7) else pattern(8, []), 1, int(b in (1, 5, 6, 7)))
                 for b in range(8)]
    pl["uq"] = [Block(at, pattern(2, []), 1, 0) for _ in range(3)]
    pl["ukv"] = [Block(at, pattern(1, []), 1, 0) for _ in range(4)]
    pl["wo"] = [Block(at, win_ada, 1, 1) for _ in range(DB)]
    pl["gu2"] = [Block(at, gu_ada0 if b == 0 else gu, 2, int(b == 0)) for b in range(FB)]
    pl["down2"] = [Block(at, pattern(22, []), 1, 0) for _ in range(DB)]
    assert at["q"] == N_MOD * DB
    tp, owner = {}, []

    def fills(name, n, by):
        tp[name] = len(owner)
        owner.extend((by * n)[:n])

    for f in ("1", "2"):
        fills("mod" + f, 8, "va")
        fills("hid" + f, 2 * (FB - 1), "v")
        fills("gate" + f, 2, "a")
        fills("hidlast" + f, 2, "v")
        fills("gateb" + f, 2, "a")
        if f == "1":
            fills("modmix", 8, "va")
            fills("qa", 2, "v")
            fills("kv", 1, "v")
            fills("kpe", 1, "v")
            fills("fqk", 8, "v")
            fills("qn", 4, "a")
            fills("kn", 4, "v")
            fills("qr", 4, "v")
            fills("pt", 2 * HEADS, "a")
            fills("gatemix", 4, "a")
    taken = [(o, owner[:n + 1].count(o)) for n, o in enumerate(owner)]
    return pl, tp, taken


def pattern_ada(n):
    return [("A", a) for a in range(n)]


def build(nc, A, const, out):
    pl, tp, taken = make_plan()
    ctx = ExitStack()
    with ctx:
        def sb(name, shape, dt=F32):
            return ctx.enter_context(nc.sbuf_tensor(name, shape, dt))

        def sem(name):
            return ctx.enter_context(nc.semaphore(name))

        raw = sb("raw", [P, RING, 2, NB])
        w_hi = sb("w_hi", [P, RING, 2, NB], F32R)
        w_lo = sb("w_lo", [P, RING, 2, NB], F32R)
        x = sb("x", [P, TT, D])
        y = sb("y", [P, TT, D])
        s = sb("s", [P, TT, NB])
        acc = sb("acc", [P, 2, NB])
        tmp = sb("tmp", [P, 2, NB])
        cst = sb("cst", [P, C_ALL])
        msk = sb("msk", [P, 3, P], BF16)
        col = sb("col", [P, V_ROWS])
        mod = sb("mod", [P, N_MOD * KD])
        a_col = sb("a_col", [P, KD])
        g_col = sb("g_col", [P, KD])
        c_col = sb("c_col", [P, 2, KD])
        ssq = sb("ssq", [P, TT, DB])
        ms = sb("ms", [P, TT])
        inv_ms = sb("inv_ms", [P, TT])
        newton = sb("newton", [P, TT])
        warm = sb("warm", [P, 1])
        rstd = sb("rstd", [P, TT])
        kpe = sb("kpe", [P, 2, TT, ROPE])
        fz = sb("fz", [P, 5, TT, HEADS])
        nmax = sb("nmax", [P, 2, TT])
        nbias = sb("nbias", [P, 2, TT])
        rsum = sb("rsum", [P, 2, TT])
        rinv = sb("rinv", [P, 2, TT])
        ident = cst[:, C_ID:C_ID + P]
        tri = cst[:, C_TRI:C_TRI + P]
        ones = cst[:, C_ONE:C_ONE + P]
        h_hi = sb("h_hi", [P, KD, SEQ], F32R)
        with nc.sbuf_tensor("gate_ffn", [P, D], F32) as gate_ffn:
            pass
        h_lo = sb("h_lo", [P, KD, SEQ], F32R)
        with ExitStack() as mix:
            def mx(name, shape, dt=F32):
                return mix.enter_context(nc.sbuf_tensor(name, shape, dt))
            qa_hi = mx("qa_hi", [P, Q_RANK // P, SEQ], F32R)
            qa_lo = mx("qa_lo", [P, Q_RANK // P, SEQ], F32R)
            ka_hi = mx("ka_hi", [P, KV_RANK // P, SEQ], F32R)
            ka_lo = mx("ka_lo", [P, KV_RANK // P, SEQ], F32R)
            fqk = mx("fqk", [P, 2 * HEADS, SEQ])
            fv = mx("fv", [P, TT, HEADS * P])
            kv = mx("kv", [P, TT, HEADS * (NOPE + DV)])
            qnT = mx("qnT", [P, HEADS, SEQ])
            knT = mx("knT", [P, HEADS, SEQ])
            qrT = mx("qrT", [P, HEADS, SEQ])
            krT = mx("krT", [P, SEQ])
            sel = mx("sel", [P, HEADS, P])
            cumT = mx("cumT", [P, SEQ])
        hid_hi = sb("hid_hi", [P, FF // P, SEQ], F32R)
        hid_lo = sb("hid_lo", [P, FF // P, SEQ], F32R)
        gate_mix = kv[:, 0, :]
        prob = y[:, 0, 0:4 * 3 * P].rearrange("p (n k) -> p n k", n=4)
        probT = y[:, 1, 0:2 * 3 * P].rearrange("p (n k) -> p n k", n=2)

        pair = [ctx.enter_context(nc.psum_tensor(f"pair{i}", [P, TT, NB], F32)) for i in range(2)]
        tps = ctx.enter_context(nc.psum_tensor("tps", [P, 2, NB], F32))
        mps = ctx.enter_context(nc.psum_tensor("mps", [P, 2, NB], F32))

        raw_landed = [sem(f"raw_landed{i}") for i in range(RING)]
        small_landed = sem("small_landed")
        x_landed = sem("x_landed")
        sel_landed = sem("sel_landed")
        out_stored = sem("out_stored")
        hi_ready = sem("hi_ready")
        raw_used = sem("raw_used")
        w_used = sem("w_used")
        evac = [sem(f"evac{i}") for i in range(2)]
        t_full = sem("t_full")
        t_taken = {"v": sem("t_taken_v"), "a": sem("t_taken_a")}
        t_hi = sem("t_hi")
        h_ready = sem("h_ready")
        sum_ready = sem("sum_ready")
        mod_ready = sem("mod_ready")
        dg_ready = sem("dg_ready")
        sq_ready = sem("sq_ready")
        ms_ready = sem("ms_ready")
        rstd_ready = sem("rstd_ready")
        ref_ready = sem("ref_ready")
        x_ready = sem("x_ready")
        xn_ready = sem("xn_ready")
        xn_ready_a = sem("xn_ready_a")
        cols_full = sem("cols_full")
        setup = sem("setup")
        c_ready = sem("c_ready")
        rot_ready = sem("rot_ready")
        fz_v = sem("fz_v")
        fz_a = sem("fz_a")
        cum_full = sem("cum_full")
        cum_ready = sem("cum_ready")
        score_full = sem("score_full")
        nbias_ready = sem("nbias_ready")
        exp_ready = sem("exp_ready")
        prob_ready = sem("prob_ready")
        o_full = sem("o_full")
        ohi_ready = sem("ohi_ready")
        o_ready = sem("o_ready")

        SMALL = 16 * 7
        doubled = [b_r for b_r in [pl["win"][1].r_of(u) for u in range(8)]]

        def landed(r, i=0, per=0):
            extra = sum(q <= r and q % RING == r % RING for q in doubled)
            return 16 * (r // RING + 1 + extra) + (i * (16 * per // RING) if per else 0)

        def plus(n, i, per):
            return n + i * per if per else n

        N_X0, N_Y1, N_X1, N_QA, N_KV, N_YM, N_XM, N_Y2 = range(8)
        SQ = {}
        n_sq = 0
        for k, n in ((N_X0, 4), (N_Y1, 8), (N_X1, 4), (N_QA, 2), (N_KV, 2), (N_YM, 8), (N_XM, 4), (N_Y2, 8)):
            SQ[k] = n_sq
            n_sq += n
        XN = {"ffn1": 0, "mix": 2, "ffn2": 4}
        HR = {"ffn1": 0, "mix": 8, "qa": 16, "kv": 18, "ffn2": 19}
        TH = {}
        n_th = 0
        for k, n in (("mod1", 8), ("hid1", 2 * FB), ("modmix", 8), ("qa", 2), ("kv", 1), ("mod2", 8), ("hid2", 2 * FB)):
            TH[k] = n_th
            n_th += n
        XB = D // 2
        DG = {"ffn1": 0, "mix": 4, "ffn2": 8}
        N_ATT = 2 * HEADS

        block = ctx.enter_context(nc.Block())

        @block.sync
        def _(sp):
            ada = A["w_ada"].rearrange("(p j) n -> p j n", j=KD)

            def load(r, src, n=NB, i=0, per=0, more=None):
                if per or r >= RING:
                    sp.wait_ge(raw_used, plus(r - RING + 1, i, per))
                sp.dma_start(raw[:, r % RING, :, 0:n], src).then_inc(raw_landed[r % RING], 16)
                if more is not None:
                    sp.dma_start(raw[:, r % RING, :, n:n + more.shape[2]], more).then_inc(raw_landed[r % RING], 16)

            def stream(b, unit, i=0, per=0, per_q=0):
                for n, (kind, u) in enumerate(b.seq):
                    if kind == "W":
                        src, cols, more = unit(u)
                        load(b.r + n, src, cols, i, per, more)
                    else:
                        c0 = plus(b.q + u // 8, i, per_q) * NB
                        j = 2 * (u % 8)
                        load(b.r + n, ada[:, j:j + 2, bass.ds(c0, NB)], NB, i, per)

            def unit_of(w, cols, at):
                v = w.rearrange("(k p) n -> p k n", p=P)
                return lambda u: (v[:, 2 * u:2 * u + 2, bass.ds(at, cols)], cols, None)

            def gate_up(gate, up, cb):
                g, v = unit_of(gate, NB, cb * NB), unit_of(up, NB, cb * NB)
                return lambda u: g(u) if u < 8 else v(u - 8)

            for t in range(TT):
                sp.dma_start(x[:, t, :], A["x"][t * P:(t + 1) * P, :]).then_inc(x_landed, 16)
            stream(pl["pre"][0], None)
            with sp.Fori(0, 3) as i:
                stream(pl["pre"][1], None, i, 16, 2)

            for f, gu, down in (("1", "gu1", "down1"), ("2", "gu2", "down2")):
                wg, wu, wd = A[f"w{f}_gate"], A[f"w{f}_up"], A[f"w{f}_down"]
                first, second = pl[gu][0], pl[gu][1]
                stream(first, gate_up(wg, wu, 0))
                per = len(second.seq)
                with sp.Fori(0, FB - 1) as i:
                    stream(second, gate_up(wg, wu, i + 1), i, per, int(second.na > 0))
                b0, b1 = pl[down][0], pl[down][1]
                per = 2 * len(b0.seq)
                with sp.Fori(0, 2) as i:
                    stream(b0, unit_of(wd, NB, i * (2 * NB)), i, per, 4)
                    stream(b1, unit_of(wd, NB, i * (2 * NB) + NB), i, per, 4)
                if f == "2":
                    break
                w_in = A["w_in"]
                kv0 = Q_RANK
                kvn = KV_RANK + ROPE
                lg = w_in.rearrange("(k p) n -> p k n", p=P)
                for b in range(8):
                    if b == 1:
                        v = unit_of(w_in, kvn, kv0)
                        stream(pl["win"][1], lambda u: (v(u)[0], kvn, lg[:, 2 * u:2 * u + 2, IN_WIDTH - HEADS:IN_WIDTH]))
                        sp.wait_ge(w_used, pl["down1"][-1].w_end)
                        sp.dma_start(sel[:], const["sel"].rearrange("k (h p) -> k h p", h=HEADS)).then_inc(sel_landed, 16)
                    else:
                        at = 0 if b == 0 else Q_RANK + kvn + (b - 2) * NB
                        stream(pl["win"][b], unit_of(w_in, NB, at))
                for b in range(3):
                    stream(pl["uq"][b], unit_of(A["w_uq"], NB, b * NB))
                for b in range(4):
                    stream(pl["ukv"][b], unit_of(A["w_ukv"], NB, b * NB))
                b0, b1 = pl["wo"][0], pl["wo"][1]
                with sp.Fori(0, 2) as i:
                    stream(b0, unit_of(A["w_o"], NB, i * (2 * NB)), i, 2 * len(b0.seq), 2)
                    stream(b1, unit_of(A["w_o"], NB, i * (2 * NB) + NB), i, 2 * len(b0.seq), 2)

            for n in range(4):
                t, c = n // 2, slice(n % 2 * XB, (n % 2 + 1) * XB)
                sp.wait_ge(x_ready, 4 * 2 + n + 1)
                sp.dma_start(out[t * P:(t + 1) * P, c], x[:, t, c]).then_inc(out_stored, 16)
            sp.wait_ge(out_stored, 16 * 4)

        @block.scalar
        def _(act):
            def hi_unit(b, u, i=0, per=0, per_w=0, n=NB):
                r, w = b.r_of(u), b.w + u
                act.wait_ge(raw_landed[r % RING], landed(r, i, per))
                if per or w >= RING:
                    act.wait_ge(w_used, plus(w - RING + 1, i, per_w))
                nc.scalar.activation(w_hi[:, w % RING, :, 0:n], raw[:, r % RING, :, 0:n], ACT.Copy).then_inc(hi_ready, 1)

            def square_x(k):
                for n in range(4):
                    t, c = n // 2, slice(n % 2 * XB, (n % 2 + 1) * XB)
                    if k == N_X0:
                        act.wait_ge(x_landed, 16 * TT)
                    else:
                        act.wait_ge(x_ready, 4 * {N_X1: 0, N_XM: 1}[k] + n + 1)
                    place = tmp if n % 2 and k != N_X0 else s
                    if n >= 2 or k == N_X0:
                        act.drain()
                    nc.scalar.activation(place[:, :, :].rearrange("p a b -> p (a b)"), x[:, t, c], ACT.Square,
                                         accum_out=ssq[:, t, n % 2:n % 2 + 1]).then_inc(sq_ready, 1)

            def warm_root():
                nc.scalar.activation(warm[:], cst[:, C_ONE:C_ONE + 1], ACT.Sqrt)

            def normalise_tile1(k):
                act.wait_ge(ref_ready, k + 1)
                for h in range(2):
                    c = slice(h * XB, (h + 1) * XB)
                    nc.scalar.activation(y[:, 1, c], x[:, 1, c], ACT.Copy, scale=rstd[:, 1:2]).then_inc(xn_ready_a, 1)

            def root(k):
                act.wait_ge(ms_ready, k + 1)
                nc.scalar.activation(rstd[:], inv_ms[:], ACT.Sqrt).then_inc(rstd_ready, 1)

            def hi_piece(cp, dst):
                nc.scalar.activation(dst[:, 2 * cp:2 * cp + 2, :],
                                     tmp[:, cp % 2, :].rearrange("p (c t) -> p c t", c=2),
                                     ACT.Copy).then_inc(t_hi, 1)

            def hi_mod(t0, dst, n_pieces):
                for cp in range(n_pieces):
                    act.wait_ge(t_taken["v"], taken[t0 + cp][1])
                    hi_piece(cp, dst)

            def modulate(name, h0, v, between):
                t0 = tp[name]
                for cp in range(8):
                    if cp in (2, 4, 6):
                        between(cp // 2 + 1)
                    if cp % 2:
                        if cp > 1:
                            act.wait_ge(h_ready, h0 + cp - 1)
                        act.wait_ge(t_full, t0 + cp + 1)
                        for c in range(2):
                            k, half = 2 * cp + c, slice(c * SEQ, (c + 1) * SEQ)
                            ins = nc.scalar.activation(tmp[:, 1, half], tps[:, (t0 + cp) % 2, half], ACT.Identity,
                                                       bias=mod[:, v * KD + k:v * KD + k + 1], scale=a_col[:, k:k + 1])
                        ins.then_inc(t_taken["a"], 1)
                        act.wait_ge(t_taken["a"], taken[t0 + cp][1])
                    else:
                        act.wait_ge(t_taken["v"], taken[t0 + cp][1])
                    hi_piece(cp, h_hi)

            def silu(b, i=0, per_w=0, per_g=0, t_prev=None, per_t=0):
                act.wait_ge(w_used, plus(b.w + 8, i, per_w))
                if t_prev is not None:
                    act.wait_ge(t_full, plus(t_prev, i, per_t))
                for t in range(TT):
                    ins = nc.scalar.activation(s[:, t, :], pair[b.g % 2][:, t, :], ACT.Silu)
                ins.then_inc(evac[b.g % 2], 1)

            def hi_hid(t0, c0, i=0, per_t=0):
                for k in range(2):
                    act.wait_ge(t_full, plus(t0 + k + 1, i, per_t))
                    nc.scalar.activation(hid_hi[:, bass.ds(c0 + 2 * k, 2), :],
                                         tps[:, (t0 + k) % 2, :].rearrange("p (c t) -> p c t", c=2),
                                         ACT.Copy).then_inc(t_hi, 1)

            def gate_row(dst, t0, j0, n):
                for j in range(n):
                    act.wait_ge(t_full, t0 + j + 1)
                    nc.scalar.activation(dst[:, (j0 + j) * NB:(j0 + j + 1) * NB], tps[:, (t0 + j) % 2, :],
                                         ACT.Copy).then_inc(t_taken["a"], 1)

            def square_y(b, k, blk):
                act.wait_ge(w_used, b.w_end)
                act.drain()
                for t in range(TT):
                    nc.scalar.activation(s[:, t, :], pair[b.g % 2][:, t, :], ACT.Square,
                                         accum_out=ssq[:, t, blk:blk + 1]).then_inc(sq_ready, 1)

            act.dma_start(cst[:], const["cst"]).then_inc(small_landed, 16)
            act.dma_start(c_col[:, 0, :], A["c"].rearrange("o (p j) -> (o p) j", j=KD)).then_inc(small_landed, 16)
            act.dma_start(y[:, 0, 0:P], A["b_ada"].rearrange("(r c) -> r c", c=P)[0:P, :]).then_inc(small_landed, 16)
            act.dma_start(y[0:N_MOD * KD - P, 0, P:2 * P],
                          A["b_ada"].rearrange("(r c) -> r c", c=P)[P:, :]).then_inc(small_landed, 16)
            act.dma_start(y[N_MOD * KD - P:G_QA - P, 0, P:2 * P], const["gains"]).then_inc(small_landed, 16)
            act.dma_start(y[G_QA - P:V_ROWS - P, 0, P:2 * P], const["gains_a"]).then_inc(small_landed, 16)
            act.dma_start(fz[:, 0, 0, :], A["b_forget"].rearrange("(o h) -> o h", o=1).to_broadcast([P, HEADS])).then_inc(small_landed, 16)
            act.wait_ge(small_landed, SMALL)
            nc.scalar.activation(c_col[:, 1, :], c_col[:, 0, :], ACT.Silu).then_inc(c_ready, 1)
            square_x(N_X0)
            root(N_X0)
            act.wait_ge(cols_full, 1)
            normalise_tile1(N_X0)

            for f, gu, down in (("1", "gu1", "down1"), ("2", "gu2", "down2")):
                first, second = pl[gu][0], pl[gu][1]
                per, t0 = len(second.seq), tp["hid" + f]
                hi_unit(first, 0)
                hi_unit(first, 1)
                if f == "2":
                    square_x(N_XM)
                    root(N_XM)
                    normalise_tile1(N_XM)
                modulate("mod" + f, HR["ffn" + f], 0 if f == "1" else 6, lambda u: hi_unit(first, u))
                for u in range(5, 16):
                    if u == 12:
                        silu(first)
                    hi_unit(first, u)
                with act.Fori(0, FB - 1) as i:
                    for u in range(16):
                        if u == 7:
                            hi_hid(t0, i * 4, i, 2)
                        if u == 12:
                            silu(second, i, 16, 1, t0 + 2, 2)
                        hi_unit(second, u, i, per, 16)
                b0 = pl[down][0]
                hi_unit(b0, 0)
                hi_unit(b0, 1)
                gate_row(gate_ffn, tp["gate" + f], 0, 2)
                hi_hid(tp["hidlast" + f], 4 * (FB - 1))
                gate_row(gate_ffn, tp["gateb" + f], 2, 2)
                k_y = N_Y1 if f == "1" else N_Y2
                for n, b in enumerate(pl[down]):
                    for u in range(22):
                        if n == 0 and u < 2:
                            continue
                        if u == 4 and n:
                            square_y(pl[down][n - 1], k_y, n - 1)
                        hi_unit(b, u)
                warm_root()
                square_y(pl[down][-1], k_y, DB - 1)
                root(k_y)
                if f == "2":
                    break

                win = pl["win"]
                hi_unit(win[0], 0)
                hi_unit(win[0], 1)
                square_x(N_X1)
                root(N_X1)
                normalise_tile1(N_X1)
                modulate("modmix", HR["mix"], 3, lambda u: hi_unit(win[0], u))
                for u in range(5, 8):
                    hi_unit(win[0], u)

                def stage(b, dst):
                    act.wait_ge(w_used, b.w_end)
                    for t in range(TT):
                        ins = nc.scalar.activation(dst(t), pair[b.g % 2][:, t, :], ACT.Copy)
                    ins.then_inc(evac[b.g % 2], 1)

                def small_squares(b, k, n):
                    act.wait_ge(w_used, b.w_end)
                    act.drain()
                    for t in range(TT):
                        nc.scalar.activation(s[:, t, 0:n], pair[b.g % 2][:, t, 0:n], ACT.Square,
                                             accum_out=ssq[:, t, 0:1]).then_inc(sq_ready, 1)
                    root(k)

                for n in range(1, 8):
                    for u in range(8):
                        if u == 4:
                            if n == 1:
                                small_squares(win[0], N_QA, Q_RANK)
                            elif n == 2:
                                small_squares(win[1], N_KV, KV_RANK)
                            elif n <= 6:
                                act.drain()
                                if n > 3:
                                    act.wait_ge(t_full, tp["fqk"] + 2 * (n - 3))
                                stage(win[n - 1], lambda t: s[:, t, :])
                            else:
                                stage(win[6], lambda t: fv[:, t, 0:NB])
                        cols = KV_RANK + ROPE + HEADS if n == 1 else NB
                        hi_unit(win[n], u, n=cols)
                    if n == 1:
                        hi_mod(tp["qa"], qa_hi, 2)
                    if n == 2:
                        hi_mod(tp["kv"], ka_hi, 1)
                    if n == 3:
                        act.wait_ge(fz_v, 1)
                        nc.scalar.activation(fz[:, 3], fz[:, 2], ACT.Exp, scale=-1.0).then_inc(fz_a, 1)
                        act.wait_ge(fz_v, 2)
                        nc.scalar.activation(fz[:, 4], fz[:, 3], ACT.Ln).then_inc(fz_a, 1)
                uq, ukv, wo = pl["uq"], pl["ukv"], pl["wo"]
                to_q = lambda b: (lambda t: y[:, t, b * NB:(b + 1) * NB])
                to_kv = lambda b: (lambda t: kv[:, t, b * NB:(b + 1) * NB])
                hi_unit(uq[0], 0)
                hi_unit(uq[0], 1)
                hi_unit(uq[1], 0)
                hi_unit(uq[1], 1)
                stage(win[7], lambda t: fv[:, t, NB:2 * NB])
                hi_unit(uq[2], 0)
                hi_unit(uq[2], 1)
                stage(uq[0], to_q(0))
                hi_unit(ukv[0], 0)
                hi_unit(ukv[1], 0)
                stage(uq[1], to_q(1))
                hi_unit(ukv[2], 0)
                hi_unit(ukv[3], 0)
                stage(uq[2], to_q(2))
                for b in range(4):
                    hi_unit(wo[0], b)
                    stage(ukv[b], to_kv(b))
                for k in range(4):
                    act.wait_ge(t_full, tp["qn"] + k + 1)
                    nc.scalar.activation(qnT[:, 2 * k:2 * k + 2, :],
                                         tps[:, (tp["qn"] + k) % 2, :].rearrange("p (c t) -> p c t", c=2),
                                         ACT.Copy).then_inc(t_taken["a"], 1)
                for n in range(1, N_ATT + 6):
                    m = n - 6
                    if m >= 0:
                        act.wait_ge(o_full, m + 1)
                        nc.scalar.activation(h_hi[:, (m + HEADS) % N_ATT, :], mps[:, m % 2, 0:SEQ],
                                             ACT.Copy).then_inc(ohi_ready, 1)
                    m = n - 1
                    if m < N_ATT:
                        scale = FOX_SCALE if m < HEADS else MLA_SCALE
                        bank = pair[(m % 4) // 2][:, m % 2, :]
                        act.wait_ge(nbias_ready, m + 1)
                        if m >= 2:
                            act.wait_ge(prob_ready, m - 1)
                        if m >= 4:
                            act.wait_ge(t_full, tp["pt"] + m - 3)
                        for t in range(TT):
                            k0, k1 = (0, P) if t == 0 else (P, 3 * P)
                            ins = nc.scalar.activation(prob[:, m % 4, k0:k1], bank[:, k0:k1], ACT.Exp,
                                                       bias=nbias[:, m % 2, t:t + 1], scale=scale,
                                                       accum_out=rsum[:, m % 2, t:t + 1])
                        ins.then_inc(exp_ready, 1)
                    m = n - 4
                    if 0 <= m < N_ATT:
                        act.wait_ge(t_full, tp["pt"] + m + 1)
                        if m >= 2:
                            act.wait_ge(o_full, m - 1)
                        nc.scalar.activation(probT[:, m % 2, :], tps[:, (tp["pt"] + m) % 2, 0:3 * P],
                                             ACT.Copy).then_inc(t_taken["a"], 1)
                gate_row(gate_mix, tp["gatemix"], 0, 4)
                for n, b in enumerate(wo):
                    for u in range(8):
                        if n == 0 and u < 4:
                            continue
                        if u == 4 and n:
                            square_y(wo[n - 1], N_YM, n - 1)
                        hi_unit(b, u)
                warm_root()
                square_y(wo[-1], N_YM, DB - 1)
                root(N_YM)

        @block.vector
        def _(dve):
            def lo_unit(b, u, i=0, per=0, per_w=0, n=NB):
                r, w = b.r_of(u), b.w + u
                dve.wait_ge(hi_ready, plus(w + 1, i, per_w))
                nc.vector.tensor_tensor(w_lo[:, w % RING, :, 0:n], raw[:, r % RING, :, 0:n],
                                        w_hi[:, w % RING, :, 0:n], ALU.subtract).then_inc(raw_used, 1)

            def ada_unit(b, n, a, i=0, per=0, acc=acc):
                r, q = b.r + n, a // 8
                if a % 8:
                    dve.drain()
                dve.wait_ge(raw_landed[r % RING], landed(r, i, per))
                for k in range(2):
                    j = 2 * (a % 8) + k
                    if j == 0:
                        ins = nc.vector.tensor_scalar(acc[:, q, :], raw[:, r % RING, 0, :], c_col[:, 1, 0:1],
                                                      None, ALU.mult)
                        continue
                    if k:
                        dve.drain()
                    ins = nc.vector.scalar_tensor_tensor(acc[:, q, :], raw[:, r % RING, k, :], c_col[:, 1, j:j + 1],
                                                         acc[:, q, :], ALU.mult, ALU.add)
                ins.then_inc(raw_used, 1)

            def run(b, tasks=None, i=0, per=0, per_w=0, start=0, stop=None, n=NB):
                a = b.seq.index(("W", start)) if start else 0
                z = b.seq.index(("W", stop)) if stop else len(b.seq)
                for at in range(a, z):
                    kind, u = b.seq[at]
                    if kind == "A":
                        ada_unit(b, at, u, i, per)
                        continue
                    if tasks and u in tasks:
                        tasks[u]()
                    lo_unit(b, u, i, per, per_w, n)

            def mod_columns(b, i=0, per_q=0):
                k, c0 = DB * b.na // 8, plus(DB * b.q, i, DB * per_q)
                dve.wait_ge(sum_ready, plus(b.m + 1, i, int(per_q > 0)))
                nc.vector.tensor_tensor(mod[:, bass.ds(c0, k)], mps[:, 0, 0:k], col[:, bass.ds(c0, k)],
                                        ALU.add).then_inc(mod_ready, 1)

            def power(k, width, columns):
                dve.wait_ge(sq_ready, SQ[k] + TT * columns)
                if columns > 1:
                    nc.vector.tensor_reduce(ms[:], ssq[:, :, 0:columns], AX_X, ALU.add)
                    dve.drain()
                    nc.vector.tensor_scalar(ms[:], ms[:], 1.0 / width, EPS, ALU.mult, ALU.add)
                else:
                    nc.vector.tensor_scalar(ms[:], ssq[:, :, 0], 1.0 / width, EPS, ALU.mult, ALU.add)
                dve.drain()
                nc.vector.reciprocal(inv_ms[:], ms[:]).then_inc(ms_ready, 1)

            def refine(k):
                dve.wait_ge(rstd_ready, k + 1)
                nc.vector.scalar_tensor_tensor(newton[:], rstd[:], -0.5, rstd[:], ALU.mult, ALU.mult)
                dve.drain()
                nc.vector.tensor_tensor(newton[:], newton[:], ms[:], ALU.mult)
                dve.drain()
                nc.vector.scalar_tensor_tensor(rstd[:], newton[:], 1.5, rstd[:], ALU.add, ALU.mult).then_inc(ref_ready, 1)
                dve.drain()

            def update_x(k):
                refine(k)
                for n in range(4):
                    t, c = n // 2, slice(n % 2 * XB, (n % 2 + 1) * XB)
                    nc.vector.scalar_tensor_tensor(x[:, t, c], y[:, t, c], rstd[:, t:t + 1], x[:, t, c],
                                                   ALU.mult, ALU.add).then_inc(x_ready, 1)

            def normalise_tile0(k):
                refine(k)
                for h in range(2):
                    c = slice(h * XB, (h + 1) * XB)
                    nc.vector.tensor_scalar(y[:, 0, c], x[:, 0, c], rstd[:, 0:1], None, ALU.mult).then_inc(xn_ready, 1)

            def lo_piece(th, cp, dst_hi, dst_lo):
                dve.wait_ge(t_hi, TH[th] + cp + 1)
                nc.vector.tensor_tensor(dst_lo[:, 2 * cp:2 * cp + 2, :],
                                        tmp[:, cp % 2, :].rearrange("p (c t) -> p c t", c=2),
                                        dst_hi[:, 2 * cp:2 * cp + 2, :], ALU.subtract).then_inc(h_ready, 1)

            def scale_piece(t0, cp, gain, shift):
                dve.drain()
                dve.wait_ge(t_full, t0 + cp + 1)
                for c in range(2):
                    k, half = 2 * cp + c, slice(c * SEQ, (c + 1) * SEQ)
                    out, bank = tmp[:, cp % 2, half], tps[:, (t0 + cp) % 2, half]
                    if shift is None:
                        ins = nc.vector.tensor_scalar(out, bank, gain[:, k:k + 1], None, ALU.mult)
                    else:
                        ins = nc.vector.tensor_scalar(out, bank, gain[:, k:k + 1], shift[:, k:k + 1],
                                                      ALU.mult, ALU.add)
                ins.then_inc(t_taken["v"], 1)

            def modulate(name, shift, between):
                t0 = tp[name]
                scale_piece(t0, 0, a_col, shift)
                lo_piece(name, 0, h_hi, h_lo)
                for cp in range(2, 8, 2):
                    between(cp // 2 + 1)
                    scale_piece(t0, cp, a_col, shift)
                    lo_piece(name, cp - 1, h_hi, h_lo)
                    lo_piece(name, cp, h_hi, h_lo)
                lo_piece(name, 7, h_hi, h_lo)

            def scale_and_split(name, dst_hi, dst_lo, gain, n_pieces):
                for cp in range(n_pieces):
                    scale_piece(tp[name], cp, gain, None)
                    lo_piece(name, cp, dst_hi, dst_lo)

            def gain_columns(v, pre):
                nc.vector.scalar_tensor_tensor(a_col[:], mod[:, (v + 1) * KD:(v + 2) * KD], 1.0,
                                               col[:, pre:pre + KD], ALU.add, ALU.mult)
                dve.drain()
                return mod[:, v * KD:(v + 1) * KD]

            def gate_columns(v, post, weight):
                nc.vector.scalar_tensor_tensor(g_col[:], mod[:, v * KD:(v + 1) * KD], weight,
                                               col[:, post:post + KD], ALU.mult, ALU.mult)
                dve.drain()

            def diagonals(j, t0, first=False):
                if not first:
                    dve.wait_ge(t_full, t0 + 1)
                for k in range(4):
                    ins = nc.vector.tensor_scalar(tmp[:, j % 2, k * P:(k + 1) * P], ident,
                                                  g_col[:, 4 * j + k:4 * j + k + 1], None, ALU.mult)
                ins.then_inc(dg_ready, 1)

            def hidden(b, i=0, per_w=0, per_g=0):
                g = b.g + 1
                dve.wait_ge(evac[b.g % 2], plus(b.g // 2 + 1, i, per_g))
                dve.wait_ge(w_used, plus(b.w + 16, i, per_w))
                for t in range(TT):
                    ins = nc.vector.tensor_tensor(s[:, t, :], s[:, t, :], pair[g % 2][:, t, :], ALU.mult)
                ins.then_inc(evac[g % 2], 1)

            def lo_hid(t0, th0, c0, i=0, per_t=0):
                for k in range(2):
                    dve.wait_ge(t_hi, plus(th0 + k + 1, i, per_t))
                    nc.vector.tensor_tensor(hid_lo[:, bass.ds(c0 + 2 * k, 2), :],
                                            tps[:, (t0 + k) % 2, :].rearrange("p (c t) -> p c t", c=2),
                                            hid_hi[:, bass.ds(c0 + 2 * k, 2), :],
                                            ALU.subtract).then_inc(t_taken["v"], 1)

            def evac_y(b, k, blk, gate, gate_fill):
                dve.wait_ge(t_taken["a"], taken[gate_fill][1])
                c = slice(blk * NB, (blk + 1) * NB)
                for t in range(TT):
                    dve.wait_ge(sq_ready, SQ[k] + 2 * blk + t + 1)
                    ins = nc.vector.tensor_tensor(y[:, t, c], pair[b.g % 2][:, t, :], gate[:, c], ALU.mult)
                ins.then_inc(evac[b.g % 2], 1)

            dve.wait_ge(small_landed, SMALL)
            nc.vector.tensor_copy(msk[:, 0, :], ident)
            nc.vector.tensor_copy(msk[:, 1:3, :], cst[:, C_MF:C_MF + 2 * P].rearrange("p (m q) -> p m q", m=2))
            dve.wait_ge(cols_full, 1)
            nc.vector.tensor_copy(col[:], mps[:, 1, 0:V_ROWS]).then_inc(setup, 1)
            dve.wait_ge(setup, 1)
            dve.wait_ge(c_ready, 1)
            pre = pl["pre"]
            for e, b in enumerate(pre):
                for n in range(16):
                    ada_unit(b, n, n, acc=tmp if e % 2 else acc)
                if e == 0:
                    power(N_X0, D, 2)
                    normalise_tile0(N_X0)
                else:
                    mod_columns(pre[e - 1])
            mod_columns(pre[-1])

            for f, gu, down in (("1", "gu1", "down1"), ("2", "gu2", "down2")):
                first, second = pl[gu][0], pl[gu][1]
                per, t0, th = len(second.seq), tp["hid" + f], TH["hid" + f]
                pre_v = 0 if f == "1" else 6
                lo_unit(first, 0)
                if f == "2":
                    update_x(N_YM)
                    lo_unit(first, 1)
                    mod_columns(pl["wo"][-1])
                    power(N_XM, D, 2)
                    normalise_tile0(N_XM)
                else:
                    lo_unit(first, 1)
                dve.drain()
                shift = gain_columns(pre_v, G_PRE["ffn" + f])
                modulate("mod" + f, shift, lambda u: run(first, start=u, stop=u + 1))
                run(first, start=5)
                with dve.Fori(0, FB - 1) as i:
                    def last_block():
                        hidden(first, i, 16, 1)
                        if first.na and f == "1":
                            mod_columns(first, i, 1)
                    run(second, {4: last_block, 7: lambda: lo_hid(t0, th, i * 4, i, 2)}, i, per, 16)
                b0, last = pl[down][0], pl[gu][-1]
                if f == "2":
                    mod_columns(first)
                dve.drain()
                gate_columns(pre_v + 2, G_POST["ffn" + f], 0.5)
                diagonals(0, 0, True)
                diagonals(1, 0, True)
                lo_unit(b0, 0)
                lo_unit(b0, 1)
                hidden(last)
                if f == "1":
                    mod_columns(last)
                lo_hid(tp["hidlast" + f], th + 2 * (FB - 1), 4 * (FB - 1))
                diagonals(2, tp["gate" + f])
                diagonals(3, tp["gate" + f] + 1)
                k_y = N_Y1 if f == "1" else N_Y2
                fills = [tp["gate" + f], tp["gate" + f] + 1, tp["gateb" + f], tp["gateb" + f] + 1]
                for n, b in enumerate(pl[down]):
                    def last_down(n=n):
                        if n:
                            evac_y(pl[down][n - 1], k_y, n - 1, gate_ffn, fills[n - 1])
                            if pl[down][n - 1].na:
                                mod_columns(pl[down][n - 1])
                    run(b, {4: last_down}, start=2 if n == 0 else 0)
                power(k_y, D, DB)
                evac_y(pl[down][-1], k_y, DB - 1, gate_ffn, fills[-1])
                if f == "2":
                    update_x(k_y)
                    break

                win = pl["win"]
                lo_unit(win[0], 0)
                update_x(N_Y1)
                lo_unit(win[0], 1)
                mod_columns(pl["down1"][-1])
                power(N_X1, D, 2)
                normalise_tile0(N_X1)
                shift = gain_columns(3, G_PRE["mix"])
                modulate("modmix", shift, lambda u: run(win[0], start=u, stop=u + 1))
                run(win[0], start=5)

                def take_qa():
                    b = win[0]
                    power(N_QA, Q_RANK, 1)
                    refine(N_QA)
                    for t in range(TT):
                        ins = nc.vector.tensor_scalar(y[:, t, 0:Q_RANK], pair[b.g % 2][:, t, :], rstd[:, t:t + 1],
                                                      None, ALU.mult)
                    ins.then_inc(evac[b.g % 2], 1)

                def take_kv():
                    b = win[1]
                    bank = pair[b.g % 2]
                    power(N_KV, KV_RANK, 1)
                    nc.vector.tensor_copy(kpe[:, 0], bank[:, :, KV_RANK:KV_RANK + ROPE])
                    nc.vector.tensor_tensor(fz[:, 1], bank[:, :, KV_RANK + ROPE:KV_RANK + ROPE + HEADS],
                                            fz[:, 0, 0:1, :].to_broadcast([P, TT, HEADS]), ALU.add)
                    refine(N_KV)
                    for t in range(TT):
                        ins = nc.vector.tensor_scalar(y[:, t, Q_RANK:Q_RANK + KV_RANK], bank[:, t, 0:KV_RANK],
                                                      rstd[:, t:t + 1], None, ALU.mult)
                    ins.then_inc(evac[b.g % 2], 1)
                    dve.drain()
                    nc.vector.scalar_tensor_tensor(fz[:, 2], fz[:, 1], -1.0, fz[:, 1], ALU.mult,
                                                   ALU.max).then_inc(fz_v, 1)

                def rotate(x1, x2, o1, o2, cos, sin, shape):
                    dve.drain()
                    size = shape[1] * shape[2]
                    part = [tmp[:, k // 2, (k % 2) * size:(k % 2 + 1) * size].rearrange("p (a b) -> p a b", a=shape[1])
                            for k in range(4)]
                    for k, (u, v) in enumerate(((x1, cos), (x2, sin), (x1, sin), (x2, cos))):
                        nc.vector.tensor_tensor(part[k], u, v, ALU.mult)
                    dve.drain()
                    nc.vector.tensor_tensor(o1, part[0], part[1], ALU.subtract)
                    return nc.vector.tensor_tensor(o2, part[2], part[3], ALU.add)

                half = ROPE // 2
                cos = cst[:, C_COS:C_COS + TT * half].rearrange("p (t e) -> p t e", t=TT)
                sin = cst[:, C_SIN:C_SIN + TT * half].rearrange("p (t e) -> p t e", t=TT)

                def copy_fill(n, dst, rows=P, width=2):
                    dve.wait_ge(t_full, n + 1)
                    src = tps[0:rows, n % 2, 0:width * SEQ]
                    if width > 1:
                        src = src.rearrange("p (c t) -> p c t", c=width)
                    nc.vector.tensor_copy(dst, src).then_inc(t_taken["v"], 1)

                for n in range(1, 8):
                    tasks = {}
                    if win[n - 1].na:
                        tasks[3] = lambda n=n: mod_columns(win[n - 1])
                    if n == 1:
                        tasks[4] = take_qa
                    if n == 2:
                        tasks[4] = take_kv
                    run(win[n], tasks, n=KV_RANK + ROPE + HEADS if n == 1 else NB)
                    if n == 1:
                        scale_and_split("qa", qa_hi, qa_lo, col[:, G_QA:G_QA + 4], 2)
                    if n == 2:
                        scale_and_split("kv", ka_hi, ka_lo, col[:, G_KV:G_KV + 2], 1)
                        rotate(kpe[:, 0, :, 0:half], kpe[:, 0, :, half:], kpe[:, 1, :, 0:half], kpe[:, 1, :, half:],
                               cos, sin, [P, TT, half]).then_inc(rot_ready, 1)
                    if n == 3:
                        nc.vector.memset(krT[ROPE:P, :], 0.0)
                        nc.vector.memset(qrT[ROPE:P, :, :], 0.0)
                        nc.vector.memset(cumT[:], 0.0)
                        copy_fill(tp["kpe"], krT[0:ROPE, :], ROPE, 1)
                        dve.wait_ge(fz_a, 1)
                        nc.vector.tensor_scalar(fz[:, 3], fz[:, 3], 1.0, None, ALU.add).then_inc(fz_v, 1)
                    if n == 4:
                        dve.wait_ge(fz_a, 2)
                        nc.vector.scalar_tensor_tensor(fz[:, 4], fz[:, 1], 0.0, fz[:, 4], ALU.min,
                                                       ALU.subtract).then_inc(fz_v, 1)
                    if n == 5:
                        dve.wait_ge(cum_full, 1)
                        nc.vector.tensor_copy(cumT[0:HEADS, :], mps[0:HEADS, 1, 0:SEQ]).then_inc(cum_ready, 1)
                    if 3 <= n <= 6:
                        for k in range(2):
                            h = 4 * (n - 3) + 2 * k
                            copy_fill(tp["fqk"] + 2 * (n - 3) + k, fqk[:, h:h + 2, :])
                uq, ukv, wo = pl["uq"], pl["ukv"], pl["wo"]
                lo_unit(uq[0], 0)
                mod_columns(win[7])
                lo_unit(uq[0], 1)
                for b in uq[1:]:
                    lo_unit(b, 0)
                    lo_unit(b, 1)
                for b in ukv:
                    lo_unit(b, 0)
                dve.wait_ge(evac[uq[2].g % 2], uq[2].g // 2 + 1)
                for t in range(TT):
                    q = y[:, t, 0:HEADS * QK].rearrange("p (h e) -> p h e", h=HEADS)
                    q1, q2 = q[:, :, NOPE:NOPE + half], q[:, :, NOPE + half:QK]
                    c, d = (v[:, t:t + 1, :].to_broadcast([P, HEADS, half]) for v in (cos, sin))
                    rotate(q1, q2, q1, q2, c, d, [P, HEADS, half]).then_inc(rot_ready, 1)
                run(wo[0], stop=4)
                for k in range(4):
                    copy_fill(tp["kn"] + k, knT[:, 2 * k:2 * k + 2, :])
                for k in range(4):
                    copy_fill(tp["qr"] + k, qrT[0:ROPE, 2 * k:2 * k + 2, :], ROPE)

                for n in range(N_ATT + 6):
                    if n < N_ATT:
                        bank = pair[(n % 4) // 2][:, n % 2, :]
                        dve.wait_ge(score_full, n + 1)
                        if n >= 2:
                            dve.wait_ge(exp_ready, n - 1)
                        for t in range(TT):
                            k0, k1 = (0, P) if t == 0 else (P, 3 * P)
                            nc.vector.tensor_reduce(nmax[:, n % 2, t:t + 1], bank[:, k0:k1], AX_X, ALU.max)
                        dve.drain()
                        nc.vector.tensor_scalar(nbias[:, n % 2, :], nmax[:, n % 2, :],
                                                -(FOX_SCALE if n < HEADS else MLA_SCALE), None,
                                                ALU.mult).then_inc(nbias_ready, 1)
                    m = n - 2
                    if 0 <= m < N_ATT:
                        dve.wait_ge(exp_ready, m + 1)
                        nc.vector.reciprocal(rinv[:, m % 2, :], rsum[:, m % 2, :])
                        dve.drain()
                        for t in range(TT):
                            k0, k1 = (0, P) if t == 0 else (P, 3 * P)
                            ins = nc.vector.tensor_scalar(prob[:, m % 4, k0:k1], prob[:, m % 4, k0:k1],
                                                          rinv[:, m % 2, t:t + 1], None, ALU.mult)
                        ins.then_inc(prob_ready, 1)
                    if n == N_ATT + 2:
                        gate_columns(5, G_POST["mix"], 1.0)
                        diagonals(0, 0, True)
                        diagonals(1, 0, True)
                    m = n - 6
                    if 0 <= m < N_ATT:
                        o = (m + HEADS) % N_ATT
                        dve.wait_ge(ohi_ready, m + 1)
                        nc.vector.tensor_tensor(h_lo[:, o, :], mps[:, m % 2, 0:SEQ], h_hi[:, o, :],
                                                ALU.subtract).then_inc(o_ready, 1)
                diagonals(2, tp["gatemix"])
                diagonals(3, tp["gatemix"] + 1)
                for n, b in enumerate(wo):
                    tasks = {}
                    if n:
                        tasks[3] = lambda n=n: mod_columns(wo[n - 1])
                        tasks[4] = lambda n=n: evac_y(wo[n - 1], N_YM, n - 1, gate_mix, tp["gatemix"] + n - 1)
                    run(b, tasks, start=4 if n == 0 else 0)
                power(N_YM, D, DB)
                evac_y(wo[-1], N_YM, DB - 1, gate_mix, tp["gatemix"] + DB - 1)

        @block.tensor
        def _(pe):
            def unit(b, u, lhs_hi, lhs_lo, k0, g, first, last, i=0, per=0, per_w=0, n=NB):
                r, w = b.r_of(u), b.w + u
                pe.wait_ge(raw_used, plus(r + 1, i, per))
                for kk in range(2):
                    for t in range(TT):
                        o = pair[g % 2][:, t, 0:n]
                        hi = lhs_hi[:, k0 + kk, t * P:(t + 1) * P]
                        lo = lhs_lo[:, k0 + kk, t * P:(t + 1) * P]
                        wh, wl = w_hi[:, w % RING, kk, 0:n], w_lo[:, w % RING, kk, 0:n]
                        nc.tensor.matmul(o, hi, wh, start=first and kk == 0, stop=False)
                        nc.tensor.matmul(o, hi, wl, start=False, stop=False)
                        ins = nc.tensor.matmul(o, lo, wh, start=False, stop=last and kk == 1)
                ins.then_inc(w_used, 1)

            def bank_free(g, i=0, per_g=0):
                if per_g or g >= 2:
                    pe.wait_ge(evac[g % 2], plus(g // 2, i, per_g))

            def fill_free(n):
                if n >= 2:
                    who, count = taken[n - 2]
                    pe.wait_ge(t_taken[who], count)

            def transposes(n, parts, free=True):
                if free:
                    fill_free(n)
                for k, src in enumerate(parts):
                    rows = src.shape[1]
                    ins = nc.tensor.transpose(tps[0:rows, n % 2, k * P:(k + 1) * P], src, ident)
                ins.then_inc(t_full, 1)

            def turn_x(n, k):
                for cp in range(8):
                    if cp % 4 == 0:
                        pe.wait_ge(xn_ready, k + 1 + cp // 4)
                        pe.wait_ge(xn_ready_a, k + 1 + cp // 4)
                    transposes(n + cp, [y[:, t, c * P:(c + 1) * P] for c in (2 * cp, 2 * cp + 1) for t in range(TT)])

            def turn_s(n, free=True):
                for k in range(2):
                    transposes(n + k, [s[:, t, c * P:(c + 1) * P] for c in (2 * k, 2 * k + 1) for t in range(TT)], free)

            def sum_columns(b, i=0, per=0, per_m=0, acc=acc):
                last_a = b.r + max(n for n, (kind, _) in enumerate(b.seq) if kind == "A")
                pe.wait_ge(raw_used, plus(last_a + 1, i, per))
                if per_m or b.m:
                    pe.wait_ge(mod_ready, plus(b.m, i, per_m))
                for k in range(DB * b.na // 8):
                    ins = nc.tensor.matmul(mps[:, 0, k:k + 1], acc[:, k // 4, (k % 4) * P:(k % 4 + 1) * P],
                                           ones[:, 0:1], start=True, stop=True)
                ins.then_inc(sum_ready, 1)

            def gate_rows(t0, dg0, n):
                for j in range(n):
                    pe.wait_ge(dg_ready, dg0 + j + 1)
                    fill_free(t0 + j)
                    nc.tensor.matmul(tps[:, (t0 + j) % 2, :], ones, tmp[:, (dg0 + j) % 2, :],
                                     start=True, stop=True).then_inc(t_full, 1)

            def gate_up(b, i=0, per=0, per_w=0, per_g=0, ready=None, after=None):
                for u in range(16):
                    g = b.g + u // 8
                    if u % 8 == 0:
                        bank_free(g, i, per_g)
                    if ready is not None and u < 8:
                        pe.wait_ge(h_ready, ready + u + 1)
                    unit(b, u, h_hi, h_lo, 2 * (u % 8), g, u % 8 == 0, u % 8 == 7, i, per, per_w)
                    if after is not None and u == 2:
                        after()

            pe.wait_ge(small_landed, SMALL)
            nc.tensor.transpose(mps[:, 1, 0:P], y[:, 0, 0:P], ident)
            rest = V_ROWS - P
            nc.tensor.transpose(mps[:, 1, P:V_ROWS], y[0:rest, 0, P:2 * P], cst[0:rest, 0:rest]).then_inc(cols_full, 1)
            pre = pl["pre"]
            for e, b in enumerate(pre):
                sum_columns(b, acc=tmp if e % 2 else acc)

            for f, gu, down in (("1", "gu1", "down1"), ("2", "gu2", "down2")):
                first, second = pl[gu][0], pl[gu][1]
                per, t0 = len(second.seq), tp["hid" + f]
                turn_x(tp["mod" + f], XN["ffn" + f])
                gate_up(first, ready=HR["ffn" + f])
                if first.na:
                    sum_columns(first)
                pe.wait_ge(t_taken["a"], taken[t0 - 1][1])
                with pe.Fori(0, FB - 1) as i:
                    def turn_last():
                        pe.wait_ge(evac[(first.g + 1) % 2], (first.g + 1) // 2 + 1 + i)
                        pe.wait_ge(t_taken["v"], taken[t0 - 2][1] + i * 2)
                        turn_s(t0, False)
                    gate_up(second, i, per, 16, 1, after=turn_last)
                    if second.na:
                        sum_columns(second, i, per, 1)
                last = pl[gu][-1]
                dg0 = DG["ffn" + f]
                gate_rows(tp["gate" + f], dg0, 2)
                pe.wait_ge(evac[(last.g + 1) % 2], (last.g + 1) // 2 + 1)
                turn_s(tp["hidlast" + f])
                gate_rows(tp["gateb" + f], dg0 + 2, 2)
                who, count = taken[tp["hidlast" + f] + 1]
                pe.wait_ge(t_taken[who], count)
                b0, b1 = pl[down][0], pl[down][1]
                with pe.Fori(0, 2) as i:
                    for b in (b0, b1):
                        bank_free(b.g, i, 1)
                        for u in range(22):
                            unit(b, u, hid_hi, hid_lo, 2 * u, b.g, u == 0, u == 21, i, 2 * len(b.seq), 44)
                        if b.na:
                            sum_columns(b, i, 2 * len(b.seq), 2)
                if f == "2":
                    break

                win = pl["win"]
                turn_x(tp["modmix"], XN["mix"])
                for n, b in enumerate(win):
                    bank_free(b.g)
                    for u in range(8):
                        if n == 0:
                            pe.wait_ge(h_ready, HR["mix"] + u + 1)
                        unit(b, u, h_hi, h_lo, 2 * u, b.g, u == 0, u == 7,
                             n=KV_RANK + ROPE + HEADS if n == 1 else NB)
                        if u == 5 and n:
                            prev = win[n - 1]
                            if n <= 6:
                                pe.wait_ge(evac[prev.g % 2], prev.g // 2 + 1)
                            if n == 1:
                                for k in range(2):
                                    transposes(tp["qa"] + k, [y[:, t, c * P:(c + 1) * P]
                                                              for c in (2 * k, 2 * k + 1) for t in range(TT)])
                            if n == 2:
                                transposes(tp["kv"], [y[:, t, Q_RANK + c * P:Q_RANK + (c + 1) * P]
                                                      for c in range(2) for t in range(TT)])
                            if n == 3:
                                pe.wait_ge(rot_ready, 1)
                                transposes(tp["kpe"], [kpe[:, 1, t, :] for t in range(TT)])
                            if 3 <= n <= 6:
                                turn_s(tp["fqk"] + 2 * (n - 3))
                            if n == 5:
                                pe.wait_ge(fz_v, 3)
                                lf = [fz[:, 4, t, :] for t in range(TT)]
                                nc.tensor.matmul(mps[0:HEADS, 1, 0:P], lf[0], tri, start=True, stop=True)
                                nc.tensor.matmul(mps[0:HEADS, 1, P:SEQ], lf[0], ones, start=True, stop=False)
                                nc.tensor.matmul(mps[0:HEADS, 1, P:SEQ], lf[1], tri, start=False,
                                                 stop=True).then_inc(cum_full, 1)
                    if b.na:
                        sum_columns(b)
                uq, ukv, wo = pl["uq"], pl["ukv"], pl["wo"]
                pe.wait_ge(h_ready, HR["kv"] + 1)
                for b in uq:
                    bank_free(b.g)
                    for u in range(2):
                        unit(b, u, qa_hi, qa_lo, 2 * u, b.g, u == 0, u == 1)
                for b in ukv:
                    bank_free(b.g)
                    unit(b, 0, ka_hi, ka_lo, 0, b.g, True, True)
                for k in range(4):
                    hs = (2 * k, 2 * k + 1)
                    transposes(tp["qn"] + k, [y[:, t, h * QK:h * QK + NOPE] for h in hs for t in range(TT)])
                for b in ukv[2:]:
                    pe.wait_ge(evac[b.g % 2], b.g // 2 + 1)
                for k in range(4):
                    hs = (2 * k, 2 * k + 1)
                    transposes(tp["kn"] + k, [kv[:, t, h * 2 * P:h * 2 * P + NOPE] for h in hs for t in range(TT)])
                pe.wait_ge(rot_ready, 1 + TT)
                for k in range(4):
                    hs = (2 * k, 2 * k + 1)
                    transposes(tp["qr"] + k, [y[:, t, h * QK + NOPE:(h + 1) * QK] for h in hs for t in range(TT)])

                pe.wait_ge(sel_landed, 16)
                pe.wait_ge(cum_ready, 1)
                pe.wait_ge(mod_ready, pl["win"][-1].m + 1)

                def scores(n):
                    bank = pair[(n % 4) // 2][:, n % 2, :]
                    if n >= 4:
                        pe.wait_ge(exp_ready, n - 3)
                    for t in range(TT):
                        q = slice(t * P, (t + 1) * P)
                        keys = slice(0, (t + 1) * P)
                        o = bank[:, P * t:P * t + (t + 1) * P]
                        diagonal = bank[:, P * t + t * P:P * t + (t + 1) * P]
                        if n < HEADS:
                            nc.tensor.matmul(o, fqk[:, n, q], fqk[:, HEADS + n, keys], start=True, stop=False)
                            nc.tensor.matmul(diagonal, msk[:, 0, :], msk[:, 1, :], start=False, stop=False)
                            ins = nc.tensor.matmul(o, sel[:, n, :], cumT[:, keys], start=False, stop=True)
                        else:
                            h = n - HEADS
                            nc.tensor.matmul(o, qnT[:, h, q], knT[:, h, keys], start=True, stop=False)
                            nc.tensor.matmul(diagonal, msk[:, 0, :], msk[:, 2, :], start=False, stop=False)
                            ins = nc.tensor.matmul(o, qrT[:, h, q], krT[:, keys], start=False, stop=True)
                    ins.then_inc(score_full, 1)

                def outputs(m):
                    pe.wait_ge(t_taken["a"], taken[tp["pt"] + m][1])
                    if m >= 2:
                        pe.wait_ge(o_ready, m - 1)
                    h = m % HEADS
                    if m < HEADS:
                        v = [fv[:, t, h * P:(h + 1) * P] for t in range(TT)]
                    else:
                        v = [kv[:, t, h * 2 * P + NOPE:(h + 1) * 2 * P] for t in range(TT)]
                    pt = probT[:, m % 2, :]
                    o = mps[:, m % 2, :]
                    nc.tensor.matmul(o[:, 0:P], v[0], pt[:, 0:P], start=True, stop=True)
                    nc.tensor.matmul(o[:, P:SEQ], v[0], pt[:, P:2 * P], start=True, stop=False)
                    nc.tensor.matmul(o[:, P:SEQ], v[1], pt[:, 2 * P:3 * P], start=False, stop=True).then_inc(o_full, 1)

                for n in range(N_ATT + 5):
                    if n < N_ATT:
                        if n == HEADS:
                            who, count = taken[tp["qr"] + 3]
                            pe.wait_ge(t_taken[who], count)
                        scores(n)
                    m = n - 3
                    if 0 <= m < N_ATT:
                        pe.wait_ge(prob_ready, m + 1)
                        transposes(tp["pt"] + m, [prob[:, m % 4, k * P:(k + 1) * P] for k in range(3)])
                    if n >= 5:
                        outputs(n - 5)
                gate_rows(tp["gatemix"], DG["mix"], 4)
                pe.wait_ge(o_ready, N_ATT)
                b0, b1 = wo[0], wo[1]
                with pe.Fori(0, 2) as i:
                    for b in (b0, b1):
                        bank_free(b.g, i, 1)
                        for u in range(8):
                            unit(b, u, h_hi, h_lo, 2 * u, b.g, u == 0, u == 7, i, 2 * len(b.seq), 16)
                        sum_columns(b, i, 2 * len(b.seq), 2)


_NAMES = ["x", "c", "w_ada", "b_ada", "w1_gate", "w1_up", "w1_down", "w_in", "b_forget", "w_uq", "w_ukv", "w_o",
          "w2_gate", "w2_up", "w2_down"]


def constants():
    j = np.arange(P)
    cst = np.zeros((P, C_ALL), np.float32)
    cst[:, C_ID:C_ID + P] = np.eye(P)
    cst[:, C_TRI:C_TRI + P] = j[:, None] <= j[None, :]
    cst[:, C_ONE:C_ONE + P] = 1.0
    cst[:, C_MF:C_MF + P] = np.where(j[None, :] <= j[:, None], 0.0, MASKED)
    cst[:, C_MM:C_MM + P] = np.where(j[None, :] // CHUNK <= j[:, None] // CHUNK, 0.0, MASKED)
    half = ROPE // 2
    inv = np.float32(10000.0) ** (-np.arange(half, dtype=np.float32) / np.float32(half))
    ang = np.arange(SEQ, dtype=np.float32)[:, None] * inv[None, :].astype(np.float32)
    for at, f in ((C_COS, np.cos), (C_SIN, np.sin)):
        v = f(ang.astype(np.float32)).astype(np.float32).reshape(TT, P, half)
        cst[:, at:at + TT * half] = v.transpose(1, 0, 2).reshape(P, TT * half)
    sel = np.zeros((P, HEADS, P), np.float32)
    for h in range(HEADS):
        sel[h, h, :] = -1.0 / FOX_SCALE
    return cst, sel.reshape(P, HEADS * P)


def kernel(**inputs):
    import concourse.bacc as bacc
    from concourse.bass_utils import run_bass_kernel_spmd

    nc = bacc.Bacc("TRN2", target_bir_lowering=False, num_devices=1, dynamic_dma_scratch_size=1024)
    arrays = {}

    def given(name, a):
        a = np.ascontiguousarray(a)
        arrays[f"in_{name}"] = a
        return nc.dram_tensor(f"in_{name}", a.shape, F32, kind="ExternalInput").ap()

    A = {}
    for name in _NAMES:
        a = np.asarray(inputs[name])
        A[name] = given(name, a if name == "c" else a.reshape(a.shape[1:]))
    rows = lambda names: np.concatenate([np.asarray(inputs[n]).reshape(-1, P) for n in names])
    cst, sel = constants()
    const = {
        "gains": given("gains", rows(["g_ffn1_pre", "g_ffn1_post", "g_mix_pre", "g_mix_post", "g_ffn2_pre", "g_ffn2_post"])),
        "gains_a": given("gains_a", rows(["g_q_a", "g_kv_a"])),
        "cst": given("cst", cst),
        "sel": given("sel", sel),
    }
    out = nc.dram_tensor("out", (SEQ, D), F32, kind="ExternalOutput").ap()
    build(nc, A, const, out)
    r = run_bass_kernel_spmd(nc, [arrays], core_ids=[0])
    return r.results[0]["out"].reshape(1, SEQ, D)
```

```python
from contextlib import ExitStack

import numpy as np

import concourse.bass as bass
from concourse import mybir

F32 = mybir.dt.float32
F32R = mybir.dt.float32r
BF16 = mybir.dt.bfloat16
ALU = mybir.AluOpType
ACT = mybir.ActivationFunctionType
AX_X = mybir.AxisListType.X

P = 128
SEQ = 256
TT = SEQ // P
D = 2048
KD = D // P
FF = 5632
Q_RANK, KV_RANK = 512, 256
NOPE, ROPE, DV = 128, 64, 128
HEADS = 8
CHUNK = 64
EPS = 1e-6
N_MOD = 9
IN_WIDTH = Q_RANK + KV_RANK + ROPE + 3 * HEADS * P + HEADS
NB = 512
FB = FF // NB
DB = D // NB
QK = NOPE + ROPE
MLA_SCALE = float(QK) ** -0.5
FOX_SCALE = float(P) ** -0.5
MASKED = -1e38

C_ID, C_TRI, C_ONE = 0, P, 2 * P
C_COS, C_SIN = 3 * P, 3 * P + TT * ROPE // 2
C_ALL = 3 * P + TT * ROPE
G_PRE = {"ffn1": 144, "mix": 176, "ffn2": 208}
G_POST = {"ffn1": 160, "mix": 192, "ffn2": 224}
G_QA, G_KV = 240, 244
V_ROWS = 246

RING = 4


def pattern(n_w, ada_after):
    seq = []
    for u in range(n_w):
        seq.append(("W", u))
        for _ in range(ada_after.count(u)):
            seq.append(("A", sum(k == "A" for k, _ in seq)))
    return seq


def mixed(n_a, w_before):
    seq = []
    for a in range(n_a):
        if a in w_before:
            seq.append(("W", w_before.index(a)))
        seq.append(("A", a))
    return seq


class Block:

    def __init__(self, at, seq, products, slot0=None):
        self.r, self.w, self.a, self.g, self.m = at["r"], at["w"], at["a"], at["g"], at["m"]
        self.seq = seq
        self.nw = sum(k == "W" for k, _ in seq)
        self.na = len(seq) - self.nw
        at["r"] += len(seq)
        at["w"] += self.nw
        self.w_end = at["w"]
        at["a"] += self.na
        at["g"] += products
        self.slot0 = slot0
        assert slot0 is not None or self.na % 8 == 0
        self.sums = [q for q in range(N_MOD * DB) if self.a <= 8 * q + 7 < at["a"]]
        self.slots = [self.slot_of(8 * q - self.a) for q in self.sums]
        at["m"] += bool(self.sums)

    def r_of(self, u):
        return self.r + self.seq.index(("W", u))

    def r_sums(self):
        return self.r + self.seq.index(("A", 8 * self.sums[-1] + 7 - self.a)) + 1

    def quarter(self, u):
        return (self.a + u) // 8, (self.a + u) % 8

    def slot_of(self, u):
        return u // 8 if self.slot0 is None else (self.quarter(u)[0] - self.slot0) % 2


def make_plan():
    at = dict(r=0, w=0, a=0, g=0, m=0)
    pl = {}
    pl["pre"] = [Block(at, mixed(16, [8, 10, 12, 14] if e else []), 0) for e in range(4)]
    gu_ada = pattern(16, [4, 5, 7, 8, 10, 11, 13, 14])
    gu = pattern(16, [])
    gu_ada0 = pattern(16, list(range(8, 16)))
    pl["gu1"] = [Block(at, gu_ada if b else pattern(4, []), 2) for b in range(FB)]
    pl["down1"] = [Block(at, pattern(22, list(range(4, 16))), 1, at["a"] // 8 - (n % 2)) for n in range(DB)]
    win_q = at["a"] // 8
    win_ada = [[6, 7]] + 4 * [[1, 3, 5, 6, 7]] + 3 * [[1, 3, 4, 5, 6, 7]]
    pl["win"] = [Block(at, pattern(8, after), 1, win_q) for after in win_ada]
    pl["uq"] = [Block(at, pattern(2, []), 1) for _ in range(3)]
    pl["ukv"] = [Block(at, pattern(1, []), 1) for _ in range(4)]
    pl["att"] = [Block(at, mixed(8, []), 0)]
    wo_q = at["a"] // 8 - 1
    pl["wo"] = [Block(at, pattern(8, after), 1, wo_q)
                for after in ([5, 6, 7, 7], [1, 3, 4, 5, 6, 7], [1, 3, 4, 5, 6, 7], [])]
    pl["gu2"] = [Block(at, gu_ada0 if b == 0 else gu_ada if b < 4 else gu, 2) for b in range(FB)]
    pl["down2"] = [Block(at, pattern(22, []), 1) for _ in range(DB)]
    assert at["a"] == 8 * N_MOD * DB
    tp, owner = {}, []

    def fills(name, n, by):
        tp[name] = len(owner)
        owner.extend((by * n)[:n])

    for f in ("1", "2"):
        fills("mod" + f, 8, "aaaaaava" if f == "1" else "va")
        fills("hid" + f, 2 * (FB - 1), "v")
        fills("gate" + f, 4, "a")
        fills("hidlast" + f, 2, "v")
        if f == "1":
            fills("modmix", 8, "va")
            fills("qa", 2, "v")
            fills("kv", 1, "v")
            fills("kpe", 1, "v")
            fills("fqk", 8, "v")
            fills("qn", 4, "a")
            fills("kn", 4, "v")
            fills("qr", 4, "v")
            fills("pt", 2 * HEADS, "a")
            fills("gatemix", 4, "a")
    taken = [(o, owner[:n + 1].count(o)) for n, o in enumerate(owner)]
    return pl, tp, taken


def build(nc, A, const, out):
    pl, tp, taken = make_plan()
    ctx = ExitStack()
    with ctx:
        def sb(name, shape, dt=F32):
            return ctx.enter_context(nc.sbuf_tensor(name, shape, dt))

        def sem(name):
            return ctx.enter_context(nc.semaphore(name))

        raw = sb("raw", [P, RING, 2, NB])
        w_hi = sb("w_hi", [P, RING, 2, NB], F32R)
        w_lo = sb("w_lo", [P, RING, 2, NB], F32R)
        x = sb("x", [P, TT, D])
        y = sb("y", [P, TT, D])
        s = sb("s", [P, TT, NB])
        acc = sb("acc", [P, 2, NB])
        tmp = sb("tmp", [P, 2, NB])
        cst = sb("cst", [P, C_ALL])
        msk = sb("msk", [P, 3, P], BF16)
        col = sb("col", [P, V_ROWS])
        mod = sb("mod", [P, N_MOD * KD])
        a_col = sb("a_col", [P, KD])
        g_col = sb("g_col", [P, KD])
        c_col = sb("c_col", [P, 2, KD])
        ssq = sb("ssq", [P, TT, DB])
        ms = sb("ms", [P, TT])
        inv_ms = sb("inv_ms", [P, TT])
        newton = sb("newton", [P, TT])
        warm = sb("warm", [P, 1])
        rstd = sb("rstd", [P, TT])
        kpe = sb("kpe", [P, 2, TT, ROPE])
        fz = sb("fz", [P, 5, TT, HEADS])
        nmax = sb("nmax", [P, 2, TT])
        nbias = sb("nbias", [P, 2, TT])
        rsum = sb("rsum", [P, 2, TT])
        rinv = sb("rinv", [P, 2, TT])
        ident = cst[:, C_ID:C_ID + P]
        tri = cst[:, C_TRI:C_TRI + P]
        ones = cst[:, C_ONE:C_ONE + P]
        h_hi = sb("h_hi", [P, KD, SEQ], F32R)
        h_lo = sb("h_lo", [P, KD, SEQ], F32R)
        with ExitStack() as mix:
            def mx(name, shape, dt=F32):
                return mix.enter_context(nc.sbuf_tensor(name, shape, dt))
            qa_hi = mx("qa_hi", [P, Q_RANK // P, SEQ], F32R)
            qa_lo = mx("qa_lo", [P, Q_RANK // P, SEQ], F32R)
            ka_hi = mx("ka_hi", [P, KV_RANK // P, SEQ], F32R)
            ka_lo = mx("ka_lo", [P, KV_RANK // P, SEQ], F32R)
            fqk = mx("fqk", [P, 2 * HEADS, SEQ])
            fv = mx("fv", [P, TT, HEADS * P])
            kv = mx("kv", [P, TT, HEADS * (NOPE + DV)])
            qnT = mx("qnT", [P, HEADS, SEQ])
            knT = mx("knT", [P, HEADS, SEQ])
            qrT = mx("qrT", [P, HEADS, SEQ])
            krT = mx("krT", [P, SEQ])
            sel = mx("sel", [P, HEADS, P])
            cumT = mx("cumT", [P, SEQ])
        with nc.sbuf_tensor("start_acc", [P, 2, 2, 2, NB], F32) as start_acc:
            pass
        hid_hi = sb("hid_hi", [P, FF // P, SEQ], F32R)
        hid_lo = sb("hid_lo", [P, FF // P, SEQ], F32R)
        gate_mix = kv[:, 0, :]
        gate_diag, gate_ffn = y[:, 0, :], y[:, 1, :]
        prob = y[:, 0, 0:4 * 3 * P].rearrange("p (n k) -> p n k", n=4)
        probT = y[:, 1, 0:2 * 3 * P].rearrange("p (n k) -> p n k", n=2)

        pair = [ctx.enter_context(nc.psum_tensor(f"pair{i}", [P, TT, NB], F32)) for i in range(2)]
        tps = ctx.enter_context(nc.psum_tensor("tps", [P, 2, NB], F32))
        mps = ctx.enter_context(nc.psum_tensor("mps", [P, 2, NB], F32))

        raw_landed = [sem(f"raw_landed{i}") for i in range(RING)]
        small_landed = sem("small_landed")
        x_landed = sem("x_landed")
        c_landed = sem("c_landed")
        sel_landed = sem("sel_landed")
        out_stored = sem("out_stored")
        hi_ready = sem("hi_ready")
        raw_used = sem("raw_used")
        w_used = sem("w_used")
        evac = [sem(f"evac{i}") for i in range(2)]
        t_full = sem("t_full")
        t_taken = {"v": sem("t_taken_v"), "a": sem("t_taken_a")}
        t_hi = sem("t_hi")
        h_ready = sem("h_ready")
        sum_ready = sem("sum_ready")
        mod_ready = sem("mod_ready")
        dg_ready = sem("dg_ready")
        half_used = sem("half_used")
        sq_ready = sem("sq_ready")
        xsq_ready = sem("xsq_ready")
        ms_ready = sem("ms_ready")
        rstd_ready = sem("rstd_ready")
        ref_ready = sem("ref_ready")
        x_ready = sem("x_ready")
        xn_ready = sem("xn_ready")
        xn_ready_a = sem("xn_ready_a")
        cols_full = sem("cols_full")
        setup = sem("setup")
        c_ready = sem("c_ready")
        gain_ready = sem("gain_ready")
        rot_ready = sem("rot_ready")
        fz_v = sem("fz_v")
        fz_a = sem("fz_a")
        cum_full = sem("cum_full")
        cum_ready = sem("cum_ready")
        score_full = sem("score_full")
        nbias_ready = sem("nbias_ready")
        exp_ready = sem("exp_ready")
        prob_ready = sem("prob_ready")
        o_full = sem("o_full")
        ohi_ready = sem("ohi_ready")
        o_ready = sem("o_ready")

        SMALL = 16 * 7
        doubled = [pl["win"][1].r_of(u) for u in range(8)]

        def landed(r, i=0, per=0):
            extra = sum(q <= r and q % RING == r % RING for q in doubled)
            return 16 * (r // RING + 1 + extra) + (i * (16 * per // RING) if per else 0)

        def plus(n, i, per):
            return n + i * per if per else n

        N_X0, N_Y1, N_X1, N_QA, N_KV, N_YM, N_XM, N_Y2 = 0, 1, 3, 4, 5, 6, 8, 9
        SQ = {N_Y1: 0, N_QA: 8, N_KV: 10, N_YM: 12, N_Y2: 20}
        XSQ = {N_X0: 0, N_X1: 4, N_XM: 8}
        XN = {"ffn1": 0, "mix": DB, "ffn2": 2 * DB}
        HR = {"ffn1": 0, "mix": 8, "qa": 16, "kv": 18, "ffn2": 19}
        TH = {}
        n_th = 0
        for k, n in (("mod1", 8), ("hid1", 2 * FB), ("modmix", 8), ("qa", 2), ("kv", 1), ("mod2", 8), ("hid2", 2 * FB)):
            TH[k] = n_th
            n_th += n
        XB = D // 2
        DG = {"ffn1": 0, "mix": 4, "ffn2": 8}
        N_ATT = 2 * HEADS
        RUNS = {"gu1": ((1, 1), (2, FB - 2)), "gu2": ((1, 3), (4, FB - 4))}

        block = ctx.enter_context(nc.Block())

        @block.sync
        def _(sp):
            ada = A["w_ada"].rearrange("(p j) n -> p j n", j=KD)

            def load(r, src, n=NB, i=0, per=0, more=None):
                if per or r >= RING:
                    sp.wait_ge(raw_used, plus(r - RING + 1, i, per))
                sp.dma_start(raw[:, r % RING, :, 0:n], src).then_inc(raw_landed[r % RING], 16)
                if more is not None:
                    sp.dma_start(raw[:, r % RING, :, n:n + more.shape[2]], more).then_inc(raw_landed[r % RING], 16)

            def stream(b, unit, i=0, per=0, per_q=0):
                for n, (kind, u) in enumerate(b.seq):
                    if kind == "W":
                        src, cols, more = unit(u)
                        load(b.r + n, src, cols, i, per, more)
                    else:
                        q, j = b.quarter(u)
                        c0, j = plus(q, i, per_q) * NB, 2 * j
                        load(b.r + n, ada[:, j:j + 2, bass.ds(c0, NB)], NB, i, per)

            def unit_of(w, cols, at):
                v = w.rearrange("(k p) n -> p k n", p=P)
                return lambda u: (v[:, 2 * u:2 * u + 2, bass.ds(at, cols)], cols, None)

            def gate_up(gate, up, cb):
                g, v = unit_of(gate, NB, cb * NB), unit_of(up, NB, cb * NB)
                return lambda u: g(u) if u < 8 else v(u - 8)

            def load_ada(b, n, u, q, i=0, per=0):
                j, c0 = 2 * (u % 8), q * NB + u // 8 * D
                load(b.r + n, ada[:, j:j + 2, bass.ds(c0, NB)], NB, i, per)

            first, second = pl["pre"][0], pl["pre"][1]
            for n in range(16):
                load_ada(first, n, n, 0)
                if n == 5:
                    for t in range(TT):
                        sp.dma_start(x[:, t, :], A["x"][t * P:(t + 1) * P, :]).then_inc(x_landed, 16)
            with sp.Fori(0, 3) as i:
                for n, (kind, u) in enumerate(second.seq):
                    if kind == "A":
                        load_ada(second, n, u, i + 1, i, 20)
                    else:
                        w = A["w1_gate" if u < 2 else "w1_up"].rearrange("(k p) n -> p k n", p=P)
                        load(second.r + n, w[:, bass.ds(i * 4 + 2 * (u % 2), 2), 0:NB], NB, i, 20)

            for f, gu, down in (("1", "gu1", "down1"), ("2", "gu2", "down2")):
                wg, wu, wd = A[f"w{f}_gate"], A[f"w{f}_up"], A[f"w{f}_down"]
                first = pl[gu][0]
                units = gate_up(wg, wu, 0)
                stream(first, units if f == "2" else lambda u: units(6 + u % 2 + u // 2 * 8))
                for start, count in RUNS[gu]:
                    b = pl[gu][start]
                    with sp.Fori(0, count) as i:
                        stream(b, gate_up(wg, wu, i + start), i, len(b.seq), int(b.na > 0))
                b0, b1 = pl[down][0], pl[down][1]
                per = 2 * len(b0.seq)
                with sp.Fori(0, 2) as i:
                    stream(b0, unit_of(wd, NB, i * (2 * NB)), i, per, 3)
                    stream(b1, unit_of(wd, NB, i * (2 * NB) + NB), i, per, 3)
                if f == "2":
                    break
                w_in = A["w_in"]
                kv0 = Q_RANK
                kvn = KV_RANK + ROPE
                lg = w_in.rearrange("(k p) n -> p k n", p=P)
                for b in range(8):
                    if b == 1:
                        v = unit_of(w_in, kvn, kv0)
                        stream(pl["win"][1], lambda u: (v(u)[0], kvn, lg[:, 2 * u:2 * u + 2, IN_WIDTH - HEADS:IN_WIDTH]))
                        sp.wait_ge(w_used, pl["down1"][-1].w_end)
                        sp.dma_start(sel[:], const["sel"].rearrange("k (h p) -> k h p", h=HEADS)).then_inc(sel_landed, 16)
                    else:
                        at = 0 if b == 0 else Q_RANK + kvn + (b - 2) * NB
                        stream(pl["win"][b], unit_of(w_in, NB, at))
                for b in range(3):
                    stream(pl["uq"][b], unit_of(A["w_uq"], NB, b * NB))
                for b in range(4):
                    stream(pl["ukv"][b], unit_of(A["w_ukv"], NB, b * NB))
                stream(pl["att"][0], None)

                def rows_of_wo(at):
                    rows = unit_of(A["w_o"], NB, at)
                    return lambda u: rows((u + 4) % 8)
                for n, b in enumerate(pl["wo"]):
                    stream(b, rows_of_wo(n * NB))

            for n in range(4):
                t, c = n // 2, slice(n % 2 * XB, (n % 2 + 1) * XB)
                sp.wait_ge(x_ready, 4 * 2 + n + 1)
                sp.dma_start(out[t * P:(t + 1) * P, c], x[:, t, c]).then_inc(out_stored, 16)
            sp.wait_ge(out_stored, 16 * 4)

        @block.scalar
        def _(act):
            def hi_unit(b, u, i=0, per=0, per_w=0, n=NB):
                r, w = b.r_of(u), b.w + u
                act.wait_ge(raw_landed[r % RING], landed(r, i, per))
                if per or w >= RING:
                    act.wait_ge(w_used, plus(w - RING + 1, i, per_w))
                nc.scalar.activation(w_hi[:, w % RING, :, 0:n], raw[:, r % RING, :, 0:n], ACT.Copy).then_inc(hi_ready, 1)

            def square_x(k, n):
                t, c = n // 2, slice(n % 2 * XB, (n % 2 + 1) * XB)
                if k == N_X0:
                    act.wait_ge(x_landed, 16 * TT)
                else:
                    act.wait_ge(x_ready, 4 * {N_X1: 0, N_XM: 1}[k] + n + 1)
                act.drain()
                nc.scalar.activation((tmp if n % 2 else s)[:, :, :].rearrange("p a b -> p (a b)"), x[:, t, c],
                                     ACT.Square, accum_out=ssq[:, t, n % 2:n % 2 + 1]).then_inc(xsq_ready, 1)

            def warm_root():
                nc.scalar.activation(warm[:], cst[:, C_ONE:C_ONE + 1], ACT.Sqrt)

            def normalise(k, tiles=(1,)):
                act.wait_ge(ref_ready, k + 1)
                for h in range(DB):
                    c = slice(h * NB, (h + 1) * NB)
                    for t in tiles:
                        nc.scalar.activation(y[:, t, c], x[:, t, c], ACT.Copy,
                                             scale=rstd[:, t:t + 1]).then_inc(xn_ready_a if t else xn_ready, 1)

            def root(k, t=slice(0, TT)):
                act.wait_ge(ms_ready, k + 1)
                nc.scalar.activation(rstd[:, t], inv_ms[:, t], ACT.Sqrt).then_inc(rstd_ready, 1)

            def hi_piece(cp, dst):
                nc.scalar.activation(dst[:, 2 * cp:2 * cp + 2, :],
                                     tmp[:, cp % 2, :].rearrange("p (c t) -> p c t", c=2),
                                     ACT.Copy).then_inc(t_hi, 1)

            def hi_mod(name, cp, dst):
                act.wait_ge(t_taken["v"], taken[tp[name] + cp][1])
                hi_piece(cp, dst)

            def modulate(name, h0, v, b):
                for cp in range(8):
                    if cp >= 4:
                        hi_unit(b, cp)
                    modulate_piece(cp, name, h0, v)

            def modulate_piece(cp, name, h0, v):
                t0 = tp[name]
                if taken[t0 + cp][0] == "a":
                    if cp > 1:
                        act.wait_ge(h_ready, h0 + cp - 1)
                    act.wait_ge(t_full, t0 + cp + 1)
                    if name == "mod1" and cp < 6:
                        act.wait_ge(gain_ready, cp // 2 + 1)
                    for c in range(2):
                        k, half = 2 * cp + c, slice(c * SEQ, (c + 1) * SEQ)
                        ins = nc.scalar.activation(tmp[:, cp % 2, half], tps[:, (t0 + cp) % 2, half], ACT.Identity,
                                                   bias=mod[:, v * KD + k:v * KD + k + 1], scale=a_col[:, k:k + 1])
                    ins.then_inc(t_taken["a"], 1)
                    act.wait_ge(t_taken["a"], taken[t0 + cp][1])
                else:
                    act.wait_ge(t_taken["v"], taken[t0 + cp][1])
                hi_piece(cp, h_hi)

            def silu(b, i=0, per_w=0, per_g=0, t_prev=None, per_t=0, w=8):
                act.wait_ge(w_used, plus(b.w + w, i, per_w))
                if t_prev is not None:
                    act.wait_ge(t_full, plus(t_prev, i, per_t))
                for t in range(TT):
                    ins = nc.scalar.activation(s[:, t, :], pair[b.g % 2][:, t, :], ACT.Silu)
                ins.then_inc(evac[b.g % 2], 1)

            def hi_hid(t0, c0, i=0, per_t=0):
                for k in range(2):
                    act.wait_ge(t_full, plus(t0 + k + 1, i, per_t))
                    nc.scalar.activation(hid_hi[:, bass.ds(c0 + 2 * k, 2), :],
                                         tps[:, (t0 + k) % 2, :].rearrange("p (c t) -> p c t", c=2),
                                         ACT.Copy).then_inc(t_hi, 1)

            def gate_row(dst, t0, j0, n):
                for j in range(n):
                    act.wait_ge(t_full, t0 + j + 1)
                    nc.scalar.activation(dst[:, (j0 + j) * NB:(j0 + j + 1) * NB], tps[:, (t0 + j) % 2, :],
                                         ACT.Copy).then_inc(t_taken["a"], 1)

            def square_y(b, k, blk):
                act.wait_ge(w_used, b.w_end)
                act.drain()
                for t in range(TT):
                    nc.scalar.activation(s[:, t, :], pair[b.g % 2][:, t, :], ACT.Square,
                                         accum_out=ssq[:, t, blk:blk + 1]).then_inc(sq_ready, 1)

            def branch_end(b, k_y, half, k_x=None, following=None):
                warm_root()
                for t in range(TT):
                    if t == 0:
                        act.wait_ge(half_used, half)
                    else:
                        act.wait_ge(w_used, b.w_end)
                    act.drain()
                    nc.scalar.activation(s[:, t, :], pair[b.g % 2][:, t, :], ACT.Square,
                                         accum_out=ssq[:, t, DB - 1:DB]).then_inc(sq_ready, 1)
                    root(k_y + t, slice(t, t + 1))
                    if k_x is not None and t == 0:
                        hi_unit(following, 0)
                        hi_unit(following, 1)
                        square_x(k_x, 0)
                if k_x is not None:
                    square_x(k_x, 1)
                    hi_unit(following, 2)
                    hi_unit(following, 3)
                    square_x(k_x, 2)
                    square_x(k_x, 3)
                    root(k_x)

            act.dma_start(c_col[:, 0, :], A["c"].rearrange("o (p j) -> (o p) j", j=KD)).then_inc(c_landed, 16)
            act.dma_start(cst[:], const["cst"]).then_inc(small_landed, 16)
            act.dma_start(y[:, 0, 2 * P:4 * P], const["masks"]).then_inc(small_landed, 16)
            act.dma_start(y[:, 0, 0:P], A["b_ada"].rearrange("(r c) -> r c", c=P)[0:P, :]).then_inc(small_landed, 16)
            act.dma_start(y[0:N_MOD * KD - P, 0, P:2 * P],
                          A["b_ada"].rearrange("(r c) -> r c", c=P)[P:, :]).then_inc(small_landed, 16)
            act.dma_start(y[N_MOD * KD - P:G_QA - P, 0, P:2 * P], const["gains"]).then_inc(small_landed, 16)
            act.dma_start(y[G_QA - P:V_ROWS - P, 0, P:2 * P], const["gains_a"]).then_inc(small_landed, 16)
            act.dma_start(fz[:, 0, 0, :], A["b_forget"].rearrange("(o h) -> o h", o=1).to_broadcast([P, HEADS])).then_inc(small_landed, 16)
            act.wait_ge(c_landed, 16)
            nc.scalar.activation(c_col[:, 1, :], c_col[:, 0, :], ACT.Silu).then_inc(c_ready, 1)
            for n in range(4):
                square_x(N_X0, n)
            root(N_X0)
            act.wait_ge(cols_full, 1)
            normalise(N_X0, (0, 1))
            for e in range(1, 5):
                if e == 4:
                    hi_unit(pl["gu1"][0], 0)
                    hi_unit(pl["gu1"][0], 1)
                for cp in (2 * e - 2, 2 * e - 1):
                    modulate_piece(cp, "mod1", HR["ffn1"], 0)
                if e < 4:
                    for u in range(4):
                        hi_unit(pl["pre"][e], u)

            for f, gu, down in (("1", "gu1", "down1"), ("2", "gu2", "down2")):
                first = pl[gu][0]
                if f == "1":
                    hi_unit(first, 2)
                    hi_unit(first, 3)
                    silu(first, w=2)
                else:
                    normalise(N_XM)
                    modulate("mod2", HR["ffn2"], 6, first)
                    for u in range(8, 16):
                        if u == 12:
                            silu(first)
                        hi_unit(first, u)
                for start, count in RUNS[gu]:
                    b, t0 = pl[gu][start], tp["hid" + f] + 2 * (start - 1)
                    with act.Fori(0, count) as i:
                        for u in range(16):
                            if u == 7:
                                hi_hid(t0, (i + (start - 1)) * 4, i, 2)
                            if u == 12:
                                silu(b, i, 16, 1, t0 + 2, 2)
                            hi_unit(b, u, i, len(b.seq), 16)
                b0 = pl[down][0]
                hi_unit(b0, 0)
                hi_unit(b0, 1)
                gate_row(gate_ffn, tp["gate" + f], 0, 4)
                hi_hid(tp["hidlast" + f], 4 * (FB - 1))
                k_y = N_Y1 if f == "1" else N_Y2
                for n, b in enumerate(pl[down]):
                    for u in range(22):
                        if n == 0 and u < 2:
                            continue
                        if u == 4 and n:
                            square_y(pl[down][n - 1], k_y, n - 1)
                        hi_unit(b, u)
                if f == "2":
                    branch_end(pl[down][-1], k_y, 5)
                    break
                win = pl["win"]
                branch_end(pl[down][-1], k_y, 2, N_X1, win[0])

                normalise(N_X1)
                modulate("modmix", HR["mix"], 3, win[0])

                def stage(b, dst):
                    act.wait_ge(w_used, b.w_end)
                    for t in range(TT):
                        ins = nc.scalar.activation(dst(t), pair[b.g % 2][:, t, :], ACT.Copy)
                    ins.then_inc(evac[b.g % 2], 1)

                def small_squares(b, n):
                    act.wait_ge(w_used, b.w_end)
                    act.drain()
                    for t in range(TT):
                        nc.scalar.activation(s[:, t, 0:n], pair[b.g % 2][:, t, 0:n], ACT.Square,
                                             accum_out=ssq[:, t, 0:1]).then_inc(sq_ready, 1)

                for n in range(1, 8):
                    for u in range(8):
                        if (n, u) in ((2, 3), (2, 5)):
                            hi_mod("qa", u // 4, qa_hi)
                        if (n, u) == (3, 3):
                            hi_mod("kv", 0, ka_hi)
                        if (n, u) == (4, 2):
                            act.wait_ge(fz_v, 1)
                            nc.scalar.activation(fz[:, 3], fz[:, 2], ACT.Exp, scale=-1.0).then_inc(fz_a, 1)
                        if (n, u) == (5, 1):
                            act.wait_ge(fz_v, 2)
                            nc.scalar.activation(fz[:, 4], fz[:, 3], ACT.Ln).then_inc(fz_a, 1)
                        if u == 4:
                            if n == 1:
                                small_squares(win[0], Q_RANK)
                            elif n == 2:
                                small_squares(win[1], KV_RANK)
                            elif n <= 6:
                                act.drain()
                                if n > 3:
                                    act.wait_ge(t_full, tp["fqk"] + 2 * (n - 3))
                                stage(win[n - 1], lambda t: s[:, t, :])
                            else:
                                stage(win[6], lambda t: fv[:, t, 0:NB])
                        if u == 6 and n <= 2:
                            root(N_QA if n == 1 else N_KV)
                        hi_unit(win[n], u, n=KV_RANK + ROPE + HEADS if n == 1 else NB)
                uq, ukv, wo = pl["uq"], pl["ukv"], pl["wo"]
                to_q = lambda b: (lambda t: y[:, t, b * NB:(b + 1) * NB])
                to_kv = lambda b: (lambda t: kv[:, t, b * NB:(b + 1) * NB])
                hi_unit(uq[0], 0)
                hi_unit(uq[0], 1)
                hi_unit(uq[1], 0)
                hi_unit(uq[1], 1)
                stage(win[7], lambda t: fv[:, t, NB:2 * NB])
                hi_unit(uq[2], 0)
                hi_unit(uq[2], 1)
                stage(uq[0], to_q(0))
                hi_unit(ukv[0], 0)
                hi_unit(ukv[1], 0)
                stage(uq[1], to_q(1))
                hi_unit(ukv[2], 0)
                hi_unit(ukv[3], 0)
                stage(uq[2], to_q(2))
                for b in range(4):
                    stage(ukv[b], to_kv(b))
                for k in range(4):
                    act.wait_ge(t_full, tp["qn"] + k + 1)
                    nc.scalar.activation(qnT[:, 2 * k:2 * k + 2, :],
                                         tps[:, (tp["qn"] + k) % 2, :].rearrange("p (c t) -> p c t", c=2),
                                         ACT.Copy).then_inc(t_taken["a"], 1)
                for n in range(1, N_ATT + 6):
                    m = n - 6
                    if m >= 0:
                        act.wait_ge(o_full, m + 1)
                        nc.scalar.activation(h_hi[:, (m + HEADS) % N_ATT, :], mps[:, m % 2, 0:SEQ],
                                             ACT.Copy).then_inc(ohi_ready, 1)
                    m = n - 1
                    if m < N_ATT:
                        scale = FOX_SCALE if m < HEADS else MLA_SCALE
                        bank = pair[(m % 4) // 2][:, m % 2, :]
                        act.wait_ge(nbias_ready, m + 1)
                        if m >= 2:
                            act.wait_ge(prob_ready, m - 1)
                        if m >= 4:
                            act.wait_ge(t_full, tp["pt"] + m - 3)
                        for t in range(TT):
                            k0, k1 = (0, P) if t == 0 else (P, 3 * P)
                            ins = nc.scalar.activation(prob[:, m % 4, k0:k1], bank[:, k0:k1], ACT.Exp,
                                                       bias=nbias[:, m % 2, t:t + 1], scale=scale,
                                                       accum_out=rsum[:, m % 2, t:t + 1])
                        ins.then_inc(exp_ready, 1)
                    m = n - 4
                    if 0 <= m < N_ATT:
                        act.wait_ge(t_full, tp["pt"] + m + 1)
                        if m >= 2:
                            act.wait_ge(o_full, m - 1)
                        nc.scalar.activation(probT[:, m % 2, :], tps[:, (tp["pt"] + m) % 2, 0:3 * P],
                                             ACT.Copy).then_inc(t_taken["a"], 1)
                    if 0 <= n - N_ATT < 4:
                        hi_unit(wo[0], n - N_ATT)
                hi_unit(wo[0], 4)
                gate_row(gate_mix, tp["gatemix"], 0, 4)
                for n, b in enumerate(wo):
                    for u in range(8):
                        if n == 0 and u < 5:
                            continue
                        if u == 4 and n:
                            square_y(wo[n - 1], N_YM, n - 1)
                        hi_unit(b, u)
                branch_end(wo[-1], N_YM, 3, N_XM, pl["gu2"][0])

        @block.vector
        def _(dve):
            def lo_unit(b, u, i=0, per=0, per_w=0, n=NB):
                r, w = b.r_of(u), b.w + u
                dve.wait_ge(hi_ready, plus(w + 1, i, per_w))
                nc.vector.tensor_tensor(w_lo[:, w % RING, :, 0:n], raw[:, r % RING, :, 0:n],
                                        w_hi[:, w % RING, :, 0:n], ALU.subtract).then_inc(raw_used, 1)

            def ada_unit(b, n, a, i=0, per=0, start=None):
                r, q, (_, j0) = b.r + n, b.slot_of(a), b.quarter(a)
                if j0:
                    dve.drain()
                dve.wait_ge(raw_landed[r % RING], landed(r, i, per))
                for k in range(2):
                    j = 2 * j0 + k
                    total = acc[:, q, :] if start is None else start[:, q, k, :]
                    if k and start is None:
                        dve.drain()
                    if j == 0 or j == 1 and start is not None:
                        ins = nc.vector.tensor_scalar(total, raw[:, r % RING, k, :], c_col[:, 1, j:j + 1],
                                                      None, ALU.mult)
                    else:
                        ins = nc.vector.scalar_tensor_tensor(total, raw[:, r % RING, k, :], c_col[:, 1, j:j + 1],
                                                             total, ALU.mult, ALU.add)
                ins.then_inc(raw_used, 1)

            def run(b, tasks=None, i=0, per=0, per_w=0, start=0, stop=None, n=NB, before=None):
                a = b.seq.index(("W", start)) if start else 0
                z = b.seq.index(("W", stop)) if stop else len(b.seq)
                for at in range(a, z):
                    kind, u = b.seq[at]
                    if kind == "A":
                        ada_unit(b, at, u, i, per)
                        continue
                    if before is not None:
                        before(u)
                    if tasks and u in tasks:
                        tasks[u]()
                    lo_unit(b, u, i, per, per_w, n)

            def mod_columns(b, i=0, per_q=0):
                k, c0 = DB * len(b.sums), plus(DB * b.sums[0], i, DB * per_q)
                dve.wait_ge(sum_ready, plus(b.m + 1, i, int(per_q > 0)))
                if b in pl["pre"]:
                    c0 = DB * pl["pre"].index(b)
                    of = lambda v: v[:, 0:2 * KD].rearrange("p (v k) -> p v k", v=2)[:, :, c0:c0 + DB]
                    nc.vector.tensor_tensor(of(mod), mps[:, 0, 0:k].rearrange("p (v k) -> p v k", v=2), of(col),
                                            ALU.add).then_inc(mod_ready, 1)
                    return
                nc.vector.tensor_tensor(mod[:, bass.ds(c0, k)], mps[:, 0, 0:k], col[:, bass.ds(c0, k)],
                                        ALU.add).then_inc(mod_ready, 1)

            def power(k, width, columns, t=slice(0, TT)):
                if k in XSQ:
                    dve.wait_ge(xsq_ready, XSQ[k] + TT * columns)
                else:
                    n = k if k in SQ else k - 1
                    dve.wait_ge(sq_ready, SQ[n] + TT * (columns - 1) + t.stop)
                if columns > 1:
                    nc.vector.tensor_reduce(ms[:, t], ssq[:, t, 0:columns], AX_X, ALU.add)
                    dve.drain()
                    nc.vector.tensor_scalar(ms[:, t], ms[:, t], 1.0 / width, EPS, ALU.mult, ALU.add)
                else:
                    nc.vector.tensor_scalar(ms[:, t], ssq[:, t, 0], 1.0 / width, EPS, ALU.mult, ALU.add)
                dve.drain()
                nc.vector.reciprocal(inv_ms[:, t], ms[:, t]).then_inc(ms_ready, 1)

            def refine(k, t=slice(0, TT)):
                dve.wait_ge(rstd_ready, k + 1)
                r, v, m = rstd[:, t], newton[:, t], ms[:, t]
                nc.vector.scalar_tensor_tensor(v, r, -0.5, r, ALU.mult, ALU.mult)
                dve.drain()
                nc.vector.tensor_tensor(v, v, m, ALU.mult)
                dve.drain()
                nc.vector.scalar_tensor_tensor(r, v, 1.5, r, ALU.add, ALU.mult).then_inc(ref_ready, 1)
                dve.drain()

            def normalise_tile0(k):
                refine(k)
                for h in range(DB):
                    c = slice(h * NB, (h + 1) * NB)
                    nc.vector.tensor_scalar(y[:, 0, c], x[:, 0, c], rstd[:, 0:1], None, ALU.mult).then_inc(xn_ready, 1)

            def lo_piece(th, cp, dst_hi, dst_lo):
                dve.wait_ge(t_hi, TH[th] + cp + 1)
                nc.vector.tensor_tensor(dst_lo[:, 2 * cp:2 * cp + 2, :],
                                        tmp[:, cp % 2, :].rearrange("p (c t) -> p c t", c=2),
                                        dst_hi[:, 2 * cp:2 * cp + 2, :], ALU.subtract).then_inc(h_ready, 1)

            def scale_piece(t0, cp, gain, shift):
                dve.drain()
                dve.wait_ge(t_full, t0 + cp + 1)
                for c in range(2):
                    k, half = 2 * cp + c, slice(c * SEQ, (c + 1) * SEQ)
                    out, bank = tmp[:, cp % 2, half], tps[:, (t0 + cp) % 2, half]
                    if shift is None:
                        ins = nc.vector.tensor_scalar(out, bank, gain[:, k:k + 1], None, ALU.mult)
                    else:
                        ins = nc.vector.tensor_scalar(out, bank, gain[:, k:k + 1], shift[:, k:k + 1],
                                                      ALU.mult, ALU.add)
                ins.then_inc(t_taken["v"], 1)

            def modulate(name, shift, b):
                def scale(cp):
                    scale_piece(tp[name], cp, a_col, shift)

                def lo(cp):
                    lo_piece(name, cp, h_hi, h_lo)

                def weights(u):
                    run(b, start=u, stop=u + 1)
                scale(0)
                lo(0)
                scale(2)
                lo(1)
                weights(2)
                lo(2)
                weights(3)
                scale(4)
                lo(3)
                lo(4)
                weights(4)
                scale(6)
                lo(5)
                lo(6)
                weights(5)
                lo(7)
                run(b, start=6)

            def gain_columns(v, pre):
                nc.vector.scalar_tensor_tensor(a_col[:], mod[:, (v + 1) * KD:(v + 2) * KD], 1.0,
                                               col[:, pre:pre + KD], ALU.add, ALU.mult)
                dve.drain()
                return mod[:, v * KD:(v + 1) * KD]

            def gate_columns(v, post, weight):
                nc.vector.scalar_tensor_tensor(g_col[:], mod[:, v * KD:(v + 1) * KD], weight,
                                               col[:, post:post + KD], ALU.mult, ALU.mult)
                dve.drain()

            def diagonals(j, place, free=None):
                if free is not None:
                    dve.wait_ge(t_full, free + 1)
                for k in range(4):
                    ins = nc.vector.tensor_scalar(place[:, k * P:(k + 1) * P], ident,
                                                  g_col[:, 4 * j + k:4 * j + k + 1], None, ALU.mult)
                ins.then_inc(dg_ready, 1)

            def hidden(b, i=0, per_w=0, per_g=0):
                g = b.g + 1
                dve.wait_ge(evac[b.g % 2], plus(b.g // 2 + 1, i, per_g))
                dve.wait_ge(w_used, plus(b.w_end, i, per_w))
                for t in range(TT):
                    ins = nc.vector.tensor_tensor(s[:, t, :], s[:, t, :], pair[g % 2][:, t, :], ALU.mult)
                ins.then_inc(evac[g % 2], 1)

            def lo_hid(t0, th0, c0, i=0, per_t=0):
                for k in range(2):
                    dve.wait_ge(t_hi, plus(th0 + k + 1, i, per_t))
                    nc.vector.tensor_tensor(hid_lo[:, bass.ds(c0 + 2 * k, 2), :],
                                            tps[:, (t0 + k) % 2, :].rearrange("p (c t) -> p c t", c=2),
                                            hid_hi[:, bass.ds(c0 + 2 * k, 2), :],
                                            ALU.subtract).then_inc(t_taken["v"], 1)

            def evac_y(b, k, blk, gate, gate_fill, tiles=range(TT)):
                dve.wait_ge(t_taken["a"], taken[gate_fill][1])
                c = slice(blk * NB, (blk + 1) * NB)
                for t in tiles:
                    dve.wait_ge(sq_ready, SQ[k] + 2 * blk + t + 1)
                    ins = nc.vector.tensor_tensor(y[:, t, c], pair[b.g % 2][:, t, :], gate[:, c], ALU.mult)
                if t == TT - 1:
                    ins.then_inc(evac[b.g % 2], 1)

            def branch_end(b, k, gate, gate_fill, following=None):
                for t in range(TT):
                    of_t = slice(t, t + 1)
                    power(k + t, D, DB, of_t)
                    evac_y(b, k, DB - 1, gate, gate_fill, [t])
                    refine(k + t, of_t)
                    for h in range(2):
                        c = slice(h * XB, (h + 1) * XB)
                        nc.vector.scalar_tensor_tensor(x[:, t, c], y[:, t, c], rstd[:, of_t], x[:, t, c],
                                                       ALU.mult, ALU.add).then_inc(x_ready, 1)
                    if following is not None:
                        lo_unit(following, t)

            pre = pl["pre"]
            dve.wait_ge(c_ready, 1)
            for n in range(16):
                ada_unit(pre[0], n, n, start=start_acc[:, 0])
            dve.wait_ge(small_landed, SMALL)
            nc.vector.tensor_copy(msk[:, 0, :], ident)
            nc.vector.tensor_copy(msk[:, 1:3, :], y[:, 0, 2 * P:4 * P].rearrange("p (m q) -> p m q", m=2))
            dve.wait_ge(cols_full, 1)
            nc.vector.tensor_copy(col[:], mps[:, 1, 0:V_ROWS]).then_inc(setup, 1)
            dve.wait_ge(setup, 1)
            power(N_X0, D, 2)
            refine(N_X0)

            def quarter_columns(e):
                mod_columns(pre[e - 1])
                dve.drain()
                k = slice(DB * (e - 1), DB * e)
                nc.vector.scalar_tensor_tensor(a_col[:, k], mod[:, KD:2 * KD][:, k], 1.0,
                                               col[:, G_PRE["ffn1"]:G_PRE["ffn1"] + KD][:, k],
                                               ALU.add, ALU.mult).then_inc(gain_ready, 1)
                dve.drain()
                return mod[:, 0:KD]

            def last_quarter():
                shift = quarter_columns(4)
                scale_piece(tp["mod1"], 6, a_col, shift)
                lo_piece("mod1", 6, h_hi, h_lo)
                lo_piece("mod1", 7, h_hi, h_lo)

            for e in range(1, 4):
                for n, (kind, u) in enumerate(pre[e].seq):
                    if (kind, u) == ("A", 5):
                        quarter_columns(e)
                    if (kind, u) == ("W", 0):
                        lo_piece("mod1", 2 * e - 2, h_hi, h_lo)
                        lo_piece("mod1", 2 * e - 1, h_hi, h_lo)
                    if kind == "W":
                        lo_unit(pre[e], u)
                    else:
                        ada_unit(pre[e], n, u, start=start_acc[:, e % 2])

            for f, gu, down in (("1", "gu1", "down1"), ("2", "gu2", "down2")):
                first, th = pl[gu][0], TH["hid" + f]
                pre_v = 0 if f == "1" else 6
                if f == "1":
                    run(first, {2: last_quarter})
                else:
                    power(N_XM, D, 2)
                    normalise_tile0(N_XM)
                    dve.drain()
                    shift = gain_columns(6, G_PRE["ffn2"])
                    modulate("mod2", shift, first)
                for start, count in RUNS[gu]:
                    before, b, at = pl[gu][start - 1], pl[gu][start], 2 * (start - 1)
                    with dve.Fori(0, count) as i:
                        def last_block():
                            hidden(before, i, 16, 1)
                            if before.sums and (b.sums or count == 1):
                                mod_columns(before, i, 1)

                        def last_hidden():
                            lo_hid(tp["hid" + f] + at, th + at, (i + (start - 1)) * 4, i, 2)
                        run(b, {4: last_block, 7: last_hidden}, i, len(b.seq), 16)
                b0, last = pl[down][0], pl[gu][-1]
                if f == "2":
                    mod_columns(pl[gu][3])
                dve.drain()
                gate_columns(pre_v + 2, G_POST["ffn" + f], 0.5)
                for j in range(DB):
                    diagonals(j, gate_diag[:, j * NB:(j + 1) * NB])
                lo_unit(b0, 0)
                lo_unit(b0, 1)
                hidden(last)
                if f == "1":
                    mod_columns(last)
                lo_hid(tp["hidlast" + f], th + 2 * (FB - 1), 4 * (FB - 1))
                k_y = N_Y1 if f == "1" else N_Y2
                fills = [tp["gate" + f] + j for j in range(DB)]
                for n, b in enumerate(pl[down]):
                    def last_down(n=n):
                        if n:
                            evac_y(pl[down][n - 1], k_y, n - 1, gate_ffn, fills[n - 1])
                            if pl[down][n - 1].sums:
                                mod_columns(pl[down][n - 1])
                    run(b, {4: last_down}, start=2 if n == 0 else 0)
                if f == "2":
                    branch_end(pl[down][-1], k_y, gate_ffn, fills[-1])
                    break
                branch_end(pl[down][-1], k_y, gate_ffn, fills[-1], pl["win"][0])

                win = pl["win"]
                mod_columns(pl["down1"][-1])
                power(N_X1, D, 2)
                normalise_tile0(N_X1)
                shift = gain_columns(3, G_PRE["mix"])
                modulate("modmix", shift, win[0])

                def take_qa():
                    b = win[0]
                    refine(N_QA)
                    for t in range(TT):
                        ins = nc.vector.tensor_scalar(y[:, t, 0:Q_RANK], pair[b.g % 2][:, t, :], rstd[:, t:t + 1],
                                                      None, ALU.mult)
                    ins.then_inc(evac[b.g % 2], 1)

                def take_kv():
                    b = win[1]
                    bank = pair[b.g % 2]
                    nc.vector.tensor_copy(kpe[:, 0], bank[:, :, KV_RANK:KV_RANK + ROPE])
                    nc.vector.tensor_tensor(fz[:, 1], bank[:, :, KV_RANK + ROPE:KV_RANK + ROPE + HEADS],
                                            fz[:, 0, 0:1, :].to_broadcast([P, TT, HEADS]), ALU.add)
                    refine(N_KV)
                    for t in range(TT):
                        ins = nc.vector.tensor_scalar(y[:, t, Q_RANK:Q_RANK + KV_RANK], bank[:, t, 0:KV_RANK],
                                                      rstd[:, t:t + 1], None, ALU.mult)
                    ins.then_inc(evac[b.g % 2], 1)
                    dve.drain()
                    nc.vector.scalar_tensor_tensor(fz[:, 2], fz[:, 1], -1.0, fz[:, 1], ALU.mult,
                                                   ALU.max).then_inc(fz_v, 1)

                def rotate(x1, x2, o1, o2, cos, sin, shape):
                    dve.drain()
                    size = shape[1] * shape[2]
                    part = [tmp[:, k // 2, (k % 2) * size:(k % 2 + 1) * size].rearrange("p (a b) -> p a b", a=shape[1])
                            for k in range(4)]
                    for k, (u, v) in enumerate(((x1, cos), (x2, sin), (x1, sin), (x2, cos))):
                        nc.vector.tensor_tensor(part[k], u, v, ALU.mult)
                    dve.drain()
                    nc.vector.tensor_tensor(o1, part[0], part[1], ALU.subtract)
                    return nc.vector.tensor_tensor(o2, part[2], part[3], ALU.add)

                half = ROPE // 2
                cos = cst[:, C_COS:C_COS + TT * half].rearrange("p (t e) -> p t e", t=TT)
                sin = cst[:, C_SIN:C_SIN + TT * half].rearrange("p (t e) -> p t e", t=TT)

                def copy_fill(n, dst, rows=P, width=2):
                    dve.wait_ge(t_full, n + 1)
                    src = tps[0:rows, n % 2, 0:width * SEQ]
                    if width > 1:
                        src = src.rearrange("p (c t) -> p c t", c=width)
                    nc.vector.tensor_copy(dst, src).then_inc(t_taken["v"], 1)

                def before_unit(n, u):
                    if u == 3 and win[n - 1].sums:
                        mod_columns(win[n - 1])
                    if u == 2 and n >= 4:
                        if n == 4:
                            copy_fill(tp["kpe"], krT[0:ROPE, :], ROPE, 1)
                        for k in range(2):
                            h = 4 * (n - 4) + 2 * k
                            copy_fill(tp["fqk"] + h // 2, fqk[:, h:h + 2, :])
                    gain_qa, gain_kv = col[:, G_QA:G_QA + 4], col[:, G_KV:G_KV + 2]
                    if (n, u) == (1, 5):
                        power(N_QA, Q_RANK, 1)
                    if (n, u) == (1, 7):
                        take_qa()
                    if (n, u) == (2, 2):
                        scale_piece(tp["qa"], 0, gain_qa, None)
                    if (n, u) == (2, 4):
                        lo_piece("qa", 0, qa_hi, qa_lo)
                        scale_piece(tp["qa"], 1, gain_qa, None)
                    if (n, u) == (2, 5):
                        power(N_KV, KV_RANK, 1)
                    if (n, u) == (2, 6):
                        lo_piece("qa", 1, qa_hi, qa_lo)
                    if (n, u) == (2, 7):
                        take_kv()
                    if (n, u) == (3, 2):
                        scale_piece(tp["kv"], 0, gain_kv, None)
                    if (n, u) == (3, 4):
                        lo_piece("kv", 0, ka_hi, ka_lo)
                    if (n, u) == (3, 5):
                        rotate(kpe[:, 0, :, 0:half], kpe[:, 0, :, half:], kpe[:, 1, :, 0:half], kpe[:, 1, :, half:],
                               cos, sin, [P, TT, half]).then_inc(rot_ready, 1)
                    if (n, u) == (3, 6):
                        nc.vector.memset(krT[ROPE:P, :], 0.0)
                        nc.vector.memset(cumT[:], 0.0)
                    if (n, u) == (7, 6):
                        nc.vector.memset(qrT[ROPE:P, :, :], 0.0)
                    if (n, u) == (4, 5):
                        dve.wait_ge(fz_a, 1)
                        nc.vector.tensor_scalar(fz[:, 3], fz[:, 3], 1.0, None, ALU.add).then_inc(fz_v, 1)
                    if (n, u) == (5, 4):
                        dve.wait_ge(fz_a, 2)
                        nc.vector.scalar_tensor_tensor(fz[:, 4], fz[:, 1], 0.0, fz[:, 4], ALU.min,
                                                       ALU.subtract).then_inc(fz_v, 1)
                    if (n, u) == (6, 3):
                        dve.wait_ge(cum_full, 1)
                        nc.vector.tensor_copy(cumT[0:HEADS, :], mps[0:HEADS, 1, 0:SEQ]).then_inc(cum_ready, 1)

                for n in range(1, 8):
                    run(win[n], n=KV_RANK + ROPE + HEADS if n == 1 else NB, before=lambda u: before_unit(n, u))
                uq, ukv, wo = pl["uq"], pl["ukv"], pl["wo"]
                lo_unit(uq[0], 0)
                mod_columns(win[7])
                lo_unit(uq[0], 1)
                for b in uq[1:]:
                    lo_unit(b, 0)
                    lo_unit(b, 1)
                for b in ukv:
                    lo_unit(b, 0)
                dve.wait_ge(evac[uq[2].g % 2], uq[2].g // 2 + 1)
                for t in range(TT):
                    q = y[:, t, 0:HEADS * QK].rearrange("p (h e) -> p h e", h=HEADS)
                    q1, q2 = q[:, :, NOPE:NOPE + half], q[:, :, NOPE + half:QK]
                    c, d = (v[:, t:t + 1, :].to_broadcast([P, HEADS, half]) for v in (cos, sin))
                    rotate(q1, q2, q1, q2, c, d, [P, HEADS, half]).then_inc(rot_ready, 1)
                for k in range(4):
                    copy_fill(tp["kn"] + k, knT[:, 2 * k:2 * k + 2, :])
                for k in range(4):
                    copy_fill(tp["qr"] + k, qrT[0:ROPE, 2 * k:2 * k + 2, :], ROPE)

                for n in range(N_ATT + 6):
                    if n < N_ATT:
                        bank = pair[(n % 4) // 2][:, n % 2, :]
                        dve.wait_ge(score_full, n + 1)
                        if n >= 2:
                            dve.wait_ge(exp_ready, n - 1)
                        for t in range(TT):
                            k0, k1 = (0, P) if t == 0 else (P, 3 * P)
                            nc.vector.tensor_reduce(nmax[:, n % 2, t:t + 1], bank[:, k0:k1], AX_X, ALU.max)
                        dve.drain()
                        nc.vector.tensor_scalar(nbias[:, n % 2, :], nmax[:, n % 2, :],
                                                -(FOX_SCALE if n < HEADS else MLA_SCALE), None,
                                                ALU.mult).then_inc(nbias_ready, 1)
                    m = n - 2
                    if 0 <= m < N_ATT:
                        dve.wait_ge(exp_ready, m + 1)
                        nc.vector.reciprocal(rinv[:, m % 2, :], rsum[:, m % 2, :])
                        dve.drain()
                        for t in range(TT):
                            k0, k1 = (0, P) if t == 0 else (P, 3 * P)
                            ins = nc.vector.tensor_scalar(prob[:, m % 4, k0:k1], prob[:, m % 4, k0:k1],
                                                          rinv[:, m % 2, t:t + 1], None, ALU.mult)
                        ins.then_inc(prob_ready, 1)
                    if n == N_ATT + 2:
                        gate_columns(5, G_POST["mix"], 1.0)
                        diagonals(0, tmp[:, 0, :])
                        diagonals(1, tmp[:, 1, :])
                    m = n - 6
                    if 0 <= m < N_ATT:
                        o = (m + HEADS) % N_ATT
                        dve.wait_ge(ohi_ready, m + 1)
                        nc.vector.tensor_tensor(h_lo[:, o, :], mps[:, m % 2, 0:SEQ], h_hi[:, o, :],
                                                ALU.subtract).then_inc(o_ready, 1)
                    if n < N_ATT and n % 2:
                        ada_unit(pl["att"][0], n // 2, n // 2)
                    if 0 <= n - N_ATT < 4:
                        lo_unit(wo[0], n - N_ATT)
                lo_unit(wo[0], 4)
                diagonals(2, tmp[:, 0, :], tp["gatemix"])
                diagonals(3, tmp[:, 1, :], tp["gatemix"] + 1)
                for n, b in enumerate(wo):
                    tasks = {}
                    if n:
                        ada = pl["att"][0] if n == 1 else wo[n - 1]
                        if ada.sums:
                            tasks[3] = lambda ada=ada: mod_columns(ada)
                        tasks[4] = lambda n=n: evac_y(wo[n - 1], N_YM, n - 1, gate_mix, tp["gatemix"] + n - 1)
                    run(b, tasks, start=5 if n == 0 else 0)
                branch_end(wo[-1], N_YM, gate_mix, tp["gatemix"] + DB - 1, pl["gu2"][0])

        @block.tensor
        def _(pe):
            def tile_products(b, u, t, lhs_hi, lhs_lo, k0, g, first, last, n=NB):
                w = b.w + u
                for kk in range(2):
                    o = pair[g % 2][:, t, 0:n]
                    hi = lhs_hi[:, k0 + kk, t * P:(t + 1) * P]
                    lo = lhs_lo[:, k0 + kk, t * P:(t + 1) * P]
                    wh, wl = w_hi[:, w % RING, kk, 0:n], w_lo[:, w % RING, kk, 0:n]
                    nc.tensor.matmul(o, hi, wh, start=first and kk == 0, stop=False)
                    nc.tensor.matmul(o, hi, wl, start=False, stop=False)
                    ins = nc.tensor.matmul(o, lo, wh, start=False, stop=last and kk == 1)
                return ins

            def unit(b, u, lhs_hi, lhs_lo, k0, g, first, last, i=0, per=0, per_w=0, n=NB):
                pe.wait_ge(raw_used, plus(b.r_of(u) + 1, i, per))
                for t in range(TT):
                    ins = tile_products(b, u, t, lhs_hi, lhs_lo, k0, g, first, last, n)
                ins.then_inc(w_used, 1)

            def skewed_units(b, lhs_hi, lhs_lo, chunk_of, i=0, per=0):
                for t in range(TT):
                    for u in range(b.nw - 4, b.nw):
                        if t == 0:
                            pe.wait_ge(raw_used, plus(b.r_of(u) + 1, i, per))
                        ins = tile_products(b, u, t, lhs_hi, lhs_lo, chunk_of(u), b.g, False, u == b.nw - 1)
                        if t:
                            ins.then_inc(w_used, 1)
                    if t == 0:
                        ins.then_inc(half_used, 1)

            def bank_free(g, i=0, per_g=0):
                if per_g or g >= 2:
                    pe.wait_ge(evac[g % 2], plus(g // 2, i, per_g))

            def fill_free(n):
                if n >= 2:
                    who, count = taken[n - 2]
                    pe.wait_ge(t_taken[who], count)

            def transposes(n, parts, free=True):
                if free:
                    fill_free(n)
                for k, src in enumerate(parts):
                    rows = src.shape[1]
                    ins = nc.tensor.transpose(tps[0:rows, n % 2, k * P:(k + 1) * P], src, ident)
                ins.then_inc(t_full, 1)

            def turn_x(n, k, cp):
                if cp % 2 == 0:
                    pe.wait_ge(xn_ready, k + 1 + cp // 2)
                    pe.wait_ge(xn_ready_a, k + 1 + cp // 2)
                transposes(n + cp, [y[:, t, c * P:(c + 1) * P] for c in (2 * cp, 2 * cp + 1) for t in range(TT)])

            def turn_ahead(n, k, u):
                for cp in ((0, 1, 2) if u == 0 else (u + 2,)):
                    if cp < 8:
                        turn_x(n, k, cp)

            def turn_s(n, free=True):
                for k in range(2):
                    transposes(n + k, [s[:, t, c * P:(c + 1) * P] for c in (2 * k, 2 * k + 1) for t in range(TT)], free)

            def sum_columns(b, i=0, per=0, per_m=0, start=None):
                pe.wait_ge(raw_used, plus(b.r_sums(), i, per))
                if per_m or b.m:
                    pe.wait_ge(mod_ready, plus(b.m, i, per_m))
                for k in range(DB * len(b.sums)):
                    c = slice((k % 4) * P, (k % 4 + 1) * P)
                    if start is None:
                        parts = [acc[:, b.slots[k // 4], c]]
                    else:
                        parts = [start[:, k // 4, row, c] for row in range(2)]
                    for n, part in enumerate(parts):
                        ins = nc.tensor.matmul(mps[:, 0, k:k + 1], part, ones[:, 0:1], start=n == 0,
                                               stop=n == len(parts) - 1)
                ins.then_inc(sum_ready, 1)

            def gate_rows(t0, dg0, places):
                for j in range(DB):
                    pe.wait_ge(dg_ready, dg0 + j + 1)
                    fill_free(t0 + j)
                    nc.tensor.matmul(tps[:, (t0 + j) % 2, :], ones, places[j],
                                     start=True, stop=True).then_inc(t_full, 1)

            def gate_up(b, i=0, per=0, per_w=0, per_g=0, ready=None, after=None, ahead=None):
                for u in range(16):
                    if ahead is not None:
                        ahead(u)
                    g = b.g + u // 8
                    if u % 8 == 0:
                        bank_free(g, i, per_g)
                    if ready is not None and u < 8:
                        pe.wait_ge(h_ready, ready + u + 1)
                    unit(b, u, h_hi, h_lo, 2 * (u % 8), g, u % 8 == 0, u % 8 == 7, i, per, per_w)
                    if after is not None and u == 2:
                        after()

            pe.wait_ge(small_landed, SMALL)
            nc.tensor.transpose(mps[:, 1, 0:P], y[:, 0, 0:P], ident)
            rest = V_ROWS - P
            nc.tensor.transpose(mps[:, 1, P:V_ROWS], y[0:rest, 0, P:2 * P], cst[0:rest, 0:rest]).then_inc(cols_full, 1)
            pre = pl["pre"]
            sum_columns(pre[0], start=start_acc[:, 0])
            for e, b in enumerate(pre[1:] + pl["gu1"][:1]):
                for cp in (2 * e, 2 * e + 1):
                    turn_x(tp["mod1"], XN["ffn1"], cp)
                for u in range(4):
                    cp = 2 * e + u % 2
                    pe.wait_ge(h_ready, HR["ffn1"] + cp + 1)
                    unit(b, u, h_hi, h_lo, 2 * cp, u // 2, cp == 0, cp == 7)
                if b.sums:
                    sum_columns(b, start=start_acc[:, (e + 1) % 2])

            for f, gu, down in (("1", "gu1", "down1"), ("2", "gu2", "down2")):
                first, t0 = pl[gu][0], tp["hid" + f]
                if f == "2":
                    gate_up(first, ready=HR["ffn2"], ahead=lambda u: turn_ahead(tp["mod2"], XN["ffn2"], u))
                    sum_columns(first)
                pe.wait_ge(t_taken["a"], taken[t0 - 1][1])
                for start, count in RUNS[gu]:
                    before, b, at = pl[gu][start - 1], pl[gu][start], 2 * (start - 1)
                    with pe.Fori(0, count) as i:
                        def turn_last():
                            pe.wait_ge(evac[(before.g + 1) % 2], (before.g + 1) // 2 + 1 + i)
                            pe.wait_ge(t_taken["v"], taken[t0 - 2][1] + at + i * 2)
                            turn_s(t0 + at, False)
                        gate_up(b, i, len(b.seq), 16, 1, after=turn_last)
                        if b.sums:
                            sum_columns(b, i, len(b.seq), 1)
                last = pl[gu][-1]
                dg0 = DG["ffn" + f]
                gate_rows(tp["gate" + f], dg0, [gate_diag[:, j * NB:(j + 1) * NB] for j in range(DB)])
                pe.wait_ge(evac[(last.g + 1) % 2], (last.g + 1) // 2 + 1)
                turn_s(tp["hidlast" + f])
                who, count = taken[tp["hidlast" + f] + 1]
                b0, b1 = pl[down][0], pl[down][1]
                with pe.Fori(0, 2) as i:
                    for b in (b0, b1):
                        bank_free(b.g, i, 1)
                        for u in range(22 if b is b0 else 18):
                            if u == 20:
                                pe.wait_ge(t_taken[who], count)
                            unit(b, u, hid_hi, hid_lo, 2 * u, b.g, u == 0, u == 21, i, 2 * len(b.seq), 44)
                        if b is b1:
                            skewed_units(b, hid_hi, hid_lo, lambda u: 2 * u, i, 2 * len(b.seq))
                        if b.sums:
                            sum_columns(b, i, 2 * len(b.seq), 2)
                if f == "2":
                    break

                win = pl["win"]
                for n, b in enumerate(win):
                    bank_free(b.g)
                    for u in range(8):
                        if n == 0:
                            turn_ahead(tp["modmix"], XN["mix"], u)
                            pe.wait_ge(h_ready, HR["mix"] + u + 1)
                        unit(b, u, h_hi, h_lo, 2 * u, b.g, u == 0, u == 7,
                             n=KV_RANK + ROPE + HEADS if n == 1 else NB)
                        if n and u == (7 if n <= 3 else 5):
                            prev = win[n - 1]
                            if n <= 6:
                                pe.wait_ge(evac[prev.g % 2], prev.g // 2 + 1)
                            if n == 1:
                                for k in range(2):
                                    transposes(tp["qa"] + k, [y[:, t, c * P:(c + 1) * P]
                                                              for c in (2 * k, 2 * k + 1) for t in range(TT)])
                            if n == 2:
                                transposes(tp["kv"], [y[:, t, Q_RANK + c * P:Q_RANK + (c + 1) * P]
                                                      for c in range(2) for t in range(TT)])
                            if n == 3:
                                pe.wait_ge(rot_ready, 1)
                                transposes(tp["kpe"], [kpe[:, 1, t, :] for t in range(TT)])
                            if 3 <= n <= 6:
                                turn_s(tp["fqk"] + 2 * (n - 3))
                            if n == 5:
                                pe.wait_ge(fz_v, 3)
                                lf = [fz[:, 4, t, :] for t in range(TT)]
                                nc.tensor.matmul(mps[0:HEADS, 1, 0:P], lf[0], tri, start=True, stop=True)
                                nc.tensor.matmul(mps[0:HEADS, 1, P:SEQ], lf[0], ones, start=True, stop=False)
                                nc.tensor.matmul(mps[0:HEADS, 1, P:SEQ], lf[1], tri, start=False,
                                                 stop=True).then_inc(cum_full, 1)
                    if b.sums:
                        sum_columns(b)
                uq, ukv, wo = pl["uq"], pl["ukv"], pl["wo"]
                pe.wait_ge(h_ready, HR["kv"] + 1)
                for b in uq:
                    bank_free(b.g)
                    for u in range(2):
                        unit(b, u, qa_hi, qa_lo, 2 * u, b.g, u == 0, u == 1)
                for b in ukv:
                    bank_free(b.g)
                    unit(b, 0, ka_hi, ka_lo, 0, b.g, True, True)
                for k in range(4):
                    hs = (2 * k, 2 * k + 1)
                    transposes(tp["qn"] + k, [y[:, t, h * QK:h * QK + NOPE] for h in hs for t in range(TT)])
                for b in ukv[2:]:
                    pe.wait_ge(evac[b.g % 2], b.g // 2 + 1)
                for k in range(4):
                    hs = (2 * k, 2 * k + 1)
                    transposes(tp["kn"] + k, [kv[:, t, h * 2 * P:h * 2 * P + NOPE] for h in hs for t in range(TT)])
                pe.wait_ge(rot_ready, 1 + TT)
                for k in range(4):
                    hs = (2 * k, 2 * k + 1)
                    transposes(tp["qr"] + k, [y[:, t, h * QK + NOPE:(h + 1) * QK] for h in hs for t in range(TT)])

                pe.wait_ge(sel_landed, 16)
                pe.wait_ge(cum_ready, 1)
                pe.wait_ge(mod_ready, pl["win"][-1].m + 1)

                def scores(n):
                    bank = pair[(n % 4) // 2][:, n % 2, :]
                    if n >= 4:
                        pe.wait_ge(exp_ready, n - 3)
                    for t in range(TT):
                        q = slice(t * P, (t + 1) * P)
                        keys = slice(0, (t + 1) * P)
                        o = bank[:, P * t:P * t + (t + 1) * P]
                        diagonal = bank[:, P * t + t * P:P * t + (t + 1) * P]
                        if n < HEADS:
                            nc.tensor.matmul(o, fqk[:, n, q], fqk[:, HEADS + n, keys], start=True, stop=False)
                            nc.tensor.matmul(diagonal, msk[:, 0, :], msk[:, 1, :], start=False, stop=False)
                            ins = nc.tensor.matmul(o, sel[:, n, :], cumT[:, keys], start=False, stop=True)
                        else:
                            h = n - HEADS
                            nc.tensor.matmul(o, qnT[:, h, q], knT[:, h, keys], start=True, stop=False)
                            nc.tensor.matmul(diagonal, msk[:, 0, :], msk[:, 2, :], start=False, stop=False)
                            ins = nc.tensor.matmul(o, qrT[:, h, q], krT[:, keys], start=False, stop=True)
                    ins.then_inc(score_full, 1)

                def outputs(m):
                    pe.wait_ge(t_taken["a"], taken[tp["pt"] + m][1])
                    if m >= 2:
                        pe.wait_ge(o_ready, m - 1)
                    h = m % HEADS
                    if m < HEADS:
                        v = [fv[:, t, h * P:(h + 1) * P] for t in range(TT)]
                    else:
                        v = [kv[:, t, h * 2 * P + NOPE:(h + 1) * 2 * P] for t in range(TT)]
                    pt = probT[:, m % 2, :]
                    o = mps[:, m % 2, :]
                    nc.tensor.matmul(o[:, 0:P], v[0], pt[:, 0:P], start=True, stop=True)
                    nc.tensor.matmul(o[:, P:SEQ], v[0], pt[:, P:2 * P], start=True, stop=False)
                    nc.tensor.matmul(o[:, P:SEQ], v[1], pt[:, 2 * P:3 * P], start=False, stop=True).then_inc(o_full, 1)

                wo = pl["wo"]

                def rows_of_wo(u):
                    return (2 * u + HEADS) % KD

                def wo_unit(b, u):
                    unit(b, u, h_hi, h_lo, rows_of_wo(u), b.g, u == 0, u == 7)

                for n in range(N_ATT + 5):
                    if n < N_ATT:
                        if n == HEADS:
                            who, count = taken[tp["qr"] + 3]
                            pe.wait_ge(t_taken[who], count)
                        scores(n)
                    m = n - 3
                    if 0 <= m < N_ATT:
                        pe.wait_ge(prob_ready, m + 1)
                        transposes(tp["pt"] + m, [prob[:, m % 4, k * P:(k + 1) * P] for k in range(3)])
                    if n >= 5:
                        outputs(n - 5)
                    if n > N_ATT:
                        if n == N_ATT + 1:
                            bank_free(wo[0].g)
                            pe.wait_ge(exp_ready, N_ATT)
                        wo_unit(wo[0], n - N_ATT - 1)
                gate_rows(tp["gatemix"], DG["mix"], [tmp[:, j % 2, :] for j in range(DB)])
                for n, b in enumerate(wo):
                    if n:
                        bank_free(b.g)
                    for u in range(0 if n else 4, 8 if n < DB - 1 else 4):
                        if n == 0:
                            pe.wait_ge(o_ready, HEADS + 2 * (u - 4) + 2)
                        wo_unit(b, u)
                    if n == DB - 1:
                        skewed_units(b, h_hi, h_lo, rows_of_wo)
                    if n == 0 or b.sums:
                        sum_columns(b if n else pl["att"][0])


_NAMES = ["x", "c", "w_ada", "b_ada", "w1_gate", "w1_up", "w1_down", "w_in", "b_forget", "w_uq", "w_ukv", "w_o",
          "w2_gate", "w2_up", "w2_down"]


def constants():
    j = np.arange(P)
    cst = np.zeros((P, C_ALL), np.float32)
    cst[:, C_ID:C_ID + P] = np.eye(P)
    cst[:, C_TRI:C_TRI + P] = j[:, None] <= j[None, :]
    cst[:, C_ONE:C_ONE + P] = 1.0
    masks = np.zeros((P, 2 * P), np.float32)
    masks[:, 0:P] = np.where(j[None, :] <= j[:, None], 0.0, MASKED)
    masks[:, P:] = np.where(j[None, :] // CHUNK <= j[:, None] // CHUNK, 0.0, MASKED)
    half = ROPE // 2
    inv = np.float32(10000.0) ** (-np.arange(half, dtype=np.float32) / np.float32(half))
    ang = np.arange(SEQ, dtype=np.float32)[:, None] * inv[None, :].astype(np.float32)
    for at, f in ((C_COS, np.cos), (C_SIN, np.sin)):
        v = f(ang.astype(np.float32)).astype(np.float32).reshape(TT, P, half)
        cst[:, at:at + TT * half] = v.transpose(1, 0, 2).reshape(P, TT * half)
    sel = np.zeros((P, HEADS, P), np.float32)
    for h in range(HEADS):
        sel[h, h, :] = -1.0 / FOX_SCALE
    return cst, masks, sel.reshape(P, HEADS * P)


def kernel(**inputs):
    import concourse.bacc as bacc
    from concourse.bass_utils import run_bass_kernel_spmd

    nc = bacc.Bacc("TRN2", target_bir_lowering=False, num_devices=1, dynamic_dma_scratch_size=1024)
    arrays = {}

    def given(name, a):
        a = np.ascontiguousarray(a)
        arrays[f"in_{name}"] = a
        return nc.dram_tensor(f"in_{name}", a.shape, F32, kind="ExternalInput").ap()

    A = {}
    for name in _NAMES:
        a = np.asarray(inputs[name])
        A[name] = given(name, a if name == "c" else a.reshape(a.shape[1:]))
    rows = lambda names: np.concatenate([np.asarray(inputs[n]).reshape(-1, P) for n in names])
    cst, masks, sel = constants()
    const = {
        "gains": given("gains", rows(["g_ffn1_pre", "g_ffn1_post", "g_mix_pre", "g_mix_post", "g_ffn2_pre", "g_ffn2_post"])),
        "gains_a": given("gains_a", rows(["g_q_a", "g_kv_a"])),
        "cst": given("cst", cst),
        "masks": given("masks", masks),
        "sel": given("sel", sel),
    }
    out = nc.dram_tensor("out", (SEQ, D), F32, kind="ExternalOutput").ap()
    build(nc, A, const, out)
    r = run_bass_kernel_spmd(nc, [arrays], core_ids=[0])
    return r.results[0]["out"].reshape(1, SEQ, D)
```
